# Optimizing a Trainium2 kernel written in Bass

```python
import math
import jax, jax.numpy as jnp
from jax import lax
import numpy as np

D_MODEL = 1024
BATCH = 1
SEQ = 256
DEPTH = 1

CHUNK = 64
CONV_DIM = D_MODEL // 2
CONV_WIDTH = 3
ATTN_HEADS = 8
HEAD_DIM = 64
ATTN_DIM = ATTN_HEADS * HEAD_DIM
Q_BLOCK = 128
IN_SPLITS = (CONV_DIM, CONV_DIM, CONV_DIM, ATTN_DIM, ATTN_DIM, ATTN_DIM, ATTN_HEADS, D_MODEL, D_MODEL)
IN_COLS = sum(IN_SPLITS)
N_EXPERTS = 32
TOP_K = 4
D_FF = D_MODEL
SWIGLU_ALPHA = 1.702
SWIGLU_LIMIT = 7.0
ROUTE_BLOCK = 256
RMS_EPS = 1e-5

kernel_name = "hybrid_gated_conv_fox_moe_block"

def rmsnorm(x, g):
    xf = x.astype(jnp.float32)
    y = xf * lax.rsqrt(jnp.mean(xf * xf, axis=-1, keepdims=True) + RMS_EPS)
    return y.astype(x.dtype) * g

def split_cols(u):
    idx = np.cumsum(IN_SPLITS)[:-1].tolist()
    return jnp.split(u, idx, axis=-1)

def short_gated_conv(b_gate, c_gate, xc, conv_w):
    u = c_gate * xc
    S = u.shape[1]
    up = jnp.pad(u, ((0, 0), (CONV_WIDTH - 1, 0), (0, 0)))
    conv = sum(conv_w[j] * up[:, j:j + S] for j in range(CONV_WIDTH))
    return b_gate * conv

def forgetting_attention(q, k, v, logf):
    Bsz, S, H, Dh = q.shape
    nb = S // Q_BLOCK
    scale = 1.0 / math.sqrt(Dh)
    c = jnp.cumsum(logf, axis=1).transpose(0, 2, 1)
    kh = k.transpose(0, 2, 1, 3)
    vh = v.transpose(0, 2, 1, 3)
    qb = q.reshape(Bsz, nb, Q_BLOCK, H, Dh).transpose(1, 0, 3, 2, 4)
    cb = c.reshape(Bsz, H, nb, Q_BLOCK).transpose(2, 0, 1, 3)
    key_pos = jnp.arange(S)

    def block(args):
        qi, ci, i = args
        q_pos = i * Q_BLOCK + jnp.arange(Q_BLOCK)
        s = jnp.einsum('bhqd,bhkd->bhqk', qi, kh).astype(jnp.float32) * scale
        s = s + (ci[..., :, None] - c[:, :, None, :])
        s = jnp.where(key_pos[None, :] <= q_pos[:, None], s, -jnp.inf)
        p = jax.nn.softmax(s, axis=-1).astype(vh.dtype)
        return jnp.einsum('bhqk,bhkd->bhqd', p, vh)

    o = lax.map(block, (qb, cb, jnp.arange(nb)))
    return o.transpose(1, 0, 3, 2, 4).reshape(Bsz, S, H * Dh)

def moe_ffn(h, w_router, b_router, w_gate_up, b_gate_up, w_down, b_down):
    N, D = h.shape
    logits = (h @ w_router + b_router).astype(jnp.float32)
    top_val, top_idx = lax.top_k(logits, TOP_K)
    gates = jax.nn.softmax(top_val, axis=-1)
    M = N * TOP_K
    flat_e = top_idx.reshape(-1)
    flat_tok = (jnp.arange(M) // TOP_K).astype(jnp.int32)
    flat_w = gates.reshape(-1)
    order = jnp.argsort(flat_e, stable=True)
    sorted_e = flat_e[order]
    counts = jnp.bincount(flat_e, length=N_EXPERTS)
    padded = ((counts + ROUTE_BLOCK - 1) // ROUTE_BLOCK) * ROUTE_BLOCK
    start = jnp.cumsum(counts) - counts
    pend = jnp.cumsum(padded)
    pstart = pend - padded
    dest = pstart[sorted_e] + (jnp.arange(M) - start[sorted_e])
    n_blocks = -(-M // ROUTE_BLOCK) + N_EXPERTS
    P = n_blocks * ROUTE_BLOCK
    slot_tok = jnp.full((P,), N, jnp.int32).at[dest].set(flat_tok[order])
    slot_w = jnp.zeros((P,), h.dtype).at[dest].set(flat_w[order].astype(h.dtype))
    block_e = jnp.minimum(jnp.searchsorted(pend, jnp.arange(n_blocks) * ROUTE_BLOCK, side='right'), N_EXPERTS - 1)
    h_pad = jnp.concatenate([h, jnp.zeros((1, D), h.dtype)], axis=0)
    xs = h_pad[slot_tok].reshape(n_blocks, ROUTE_BLOCK, D)

    def expert_block(args):
        xb, e = args
        gu = xb @ w_gate_up[e] + b_gate_up[e]
        x_glu, x_lin = jnp.split(gu, 2, axis=-1)
        x_glu = jnp.minimum(x_glu, SWIGLU_LIMIT)
        x_lin = jnp.clip(x_lin, -SWIGLU_LIMIT, SWIGLU_LIMIT)
        act = (x_glu * jax.nn.sigmoid(SWIGLU_ALPHA * x_glu)) * (x_lin + 1.0)
        return act @ w_down[e] + b_down[e]

    ys = lax.map(expert_block, (xs, block_e)).reshape(P, D)
    out = jnp.zeros((N + 1, D), h.dtype).at[slot_tok].add(ys * slot_w[:, None])
    return out[:N]

def setup_inputs(seed: int = 0) -> dict:
    key = jax.random.key(seed)
    ks = jax.random.split(key, 16)
    f32 = jnp.float32
    nrm = lambda k, shp, s: jax.random.normal(k, shp, f32) * s
    return {
        "x": nrm(ks[0], (BATCH, SEQ, D_MODEL), 1.0),
        "g_mix": 1.0 + nrm(ks[1], (D_MODEL,), 0.02),
        "w_in": nrm(ks[2], (D_MODEL, IN_COLS), D_MODEL ** -0.5),
        "conv_w": nrm(ks[3], (CONV_WIDTH, CONV_DIM), CONV_WIDTH ** -0.5),
        "b_f": 3.0 + nrm(ks[4], (ATTN_HEADS,), 0.5),
        "w_conv_o": nrm(ks[5], (CONV_DIM, D_MODEL), CONV_DIM ** -0.5),
        "w_attn_o": nrm(ks[6], (ATTN_DIM, D_MODEL), ATTN_DIM ** -0.5),
        "w_out": nrm(ks[7], (D_MODEL, D_MODEL), D_MODEL ** -0.5),
        "g_ffn": 1.0 + nrm(ks[8], (D_MODEL,), 0.02),
        "w_router": nrm(ks[9], (D_MODEL, N_EXPERTS), D_MODEL ** -0.5),
        "b_router": nrm(ks[10], (N_EXPERTS,), 0.01),
        "w_gate_up": nrm(ks[11], (N_EXPERTS, D_MODEL, 2 * D_FF), D_MODEL ** -0.5),
        "b_gate_up": nrm(ks[12], (N_EXPERTS, 2 * D_FF), 0.01),
        "w_down": nrm(ks[13], (N_EXPERTS, D_FF, D_MODEL), D_FF ** -0.5),
        "b_down": nrm(ks[14], (N_EXPERTS, D_MODEL), 0.01),
        "g_final": 1.0 + nrm(ks[15], (D_MODEL,), 0.02),
    }

def reference(x, g_mix, w_in, conv_w, b_f, w_conv_o, w_attn_o, w_out, g_ffn, w_router, b_router, w_gate_up, b_gate_up, w_down, b_down, g_final):
    Bsz, S, D = x.shape
    for _ in range(DEPTH):
        h = rmsnorm(x, g_mix)
        u = h @ w_in
        cb, cc, cx, q, k, v, fl, gc, ga = split_cols(u)
        y_conv = short_gated_conv(cb, cc, cx, conv_w) @ w_conv_o
        logf = jax.nn.log_sigmoid((fl + b_f).astype(jnp.float32))
        hs = (Bsz, S, ATTN_HEADS, HEAD_DIM)
        o = forgetting_attention(q.reshape(hs), k.reshape(hs), v.reshape(hs), logf)
        y_attn = o @ w_attn_o
        mixed = jax.nn.sigmoid(gc) * y_conv + jax.nn.sigmoid(ga) * y_attn
        x = x + mixed @ w_out
        h2 = rmsnorm(x, g_ffn).reshape(Bsz * S, D)
        x = x + moe_ffn(h2, w_router, b_router, w_gate_up, b_gate_up, w_down, b_down).reshape(Bsz, S, D)
    return rmsnorm(x, g_final)


_drawn_inputs = setup_inputs


def setup_inputs(seed=0):
    import zlib

    import numpy as np

    out = dict(_drawn_inputs(seed))
    spreads = {}
    factors = {'b_gate_up': 8.0, 'b_down': 8.0, 'g_final': 2.861}
    for name, (base, spread) in spreads.items():
        noise = np.random.default_rng([zlib.crc32(name.encode()), seed]).standard_normal(out[name].shape)
        drawn = base * np.exp(spread * noise) if base else spread * noise
        out[name] = __import__('jax').numpy.asarray(drawn.astype(out[name].dtype))
    for name, factor in factors.items():
        out[name] = (out[name] * factor).astype(out[name].dtype)
    return out
```

```python
from contextlib import ExitStack

import concourse.bass as bass
from concourse import mybir

P = 128
D = 1024
SEQ = 256
NT = SEQ // P
KD = D // P
CONV = 512
HEADS = 8
HD = 64
ATT = HEADS * HD
E = 32
TOPK = 4
FF = 1024
LIMIT = 7.0
ALPHA = 1.702
EPS = 1e-5
NSLOT = 16
SLOT = 2048
CAP = 64
USED = 64
XROUNDS = SEQ // USED - 1
TPB = 4
XTASKS = -(-(SEQ * TOPK // (USED + 1)) // TPB) * TPB
XCOLS = XTASKS + 2
TCOLS = E + XCOLS
XBODIES = XTASKS // TPB
GROUPS = 10
MIXER_USES = 2 * GROUPS + 2 + 2 + 4
TASK_USES = 12
FREED = TASK_USES - 2
MASKED = -1e30

F32 = mybir.dt.float32
I32 = mybir.dt.int32
U32 = mybir.dt.uint32
ALU = mybir.AluOpType
ACT = mybir.ActivationFunctionType
AX = mybir.AxisListType

QK_TILES = [("q", m) for m in range(4)] + [("k", m) for m in range(4)]
V_TILES = [("v", t) for t in range(NT)]
CONV_TILES = [(w, m) for w in ("cc", "cx", "cb") for m in range(4)]
GATE_TILES = [(w, m) for w in ("gc", "ga") for m in range(KD)]
Y_TILES = [(w, m) for w in ("yc", "ya") for m in range(KD)]
X_TILES = [("x", i) for i in range(2 * NT)]
TILES = QK_TILES + V_TILES + CONV_TILES + GATE_TILES + Y_TILES + X_TILES
BY_SCALAR = ("k", "v", "cc", "gc", "ga")
GROUP_OF = {"q": 0, "k": 1, "v": 2, "cc": 3, "cx": 4, "cb": 5, "gc": 6, "ga": 8}
GROUP_COL = [1536, 2048, 2560, 512, 1024, 0, 3080, 3592, 4104, 4616]
FORGET_COL = 3072


def tiles_read(i, by_scalar):
    return sum((k in BY_SCALAR) == by_scalar for k, _ in TILES[:i + 1])


def build(nc, x, g_mix, w_in, conv_w, b_f, w_conv_o, w_attn_o, w_out, g_ffn, w_router, b_router,
          w_gate_up, b_gate_up, w_down, b_down, g_final, out):
    with ExitStack() as ctx:
        def sb(name, shape, dt=F32):
            return ctx.enter_context(nc.sbuf_tensor(name, shape, dt))

        def sem(name):
            return ctx.enter_context(nc.semaphore(name))

        ps = [ctx.enter_context(nc.psum_tensor(f"ps{i}", [P, 512], F32)) for i in range(8)]

        ring = sb("ring", [P, NSLOT, SLOT])
        x_res = sb("x_res", [P, NT, D])
        h_tok = sb("h_tok", [P, NT, D])
        h_area = sb("h_area", [P, KD * SEQ])
        qk_area = sb("qk_area", [P, 2048])
        v_area = sb("v_area", [P, NT * ATT])
        conv_area = sb("conv_area", [P, 4 * SEQ + 4 * (SEQ + 2)])
        gc_area = sb("gc_area", [P, KD * SEQ])
        ga_area = sb("ga_area", [P, KD * SEQ])
        o_area = sb("o_area", [P, 4 * SEQ])
        gain = sb("gain", [P, 2, D])

        hT = h_area[:, :].rearrange("p (k n) -> p k n", k=KD)
        qT = qk_area[:, 0:1024].rearrange("p (m n) -> p m n", m=4)
        kT = qk_area[:, 1024:2048].rearrange("p (m n) -> p m n", m=4)
        v_tok = v_area[:, :].rearrange("p (t n) -> p t n", t=NT)
        cc = conv_area[:, 0:1024].rearrange("p (m n) -> p m n", m=4)
        u_pad = conv_area[:, 1024:].rearrange("p (m n) -> p m n", m=4)
        gate_c = gc_area[:, :].rearrange("p (k n) -> p k n", k=KD)
        gate_a = ga_area[:, :].rearrange("p (k n) -> p k n", k=KD)
        oT = o_area[:, :].rearrange("p (m n) -> p m n", m=4)
        s_sb = [ga_area[:, 256 * t:256 * t + 256] for t in range(NT)]
        p_sb = [ga_area[:, 512 + 256 * t:768 + 256 * t] for t in range(NT)]
        pT_sb = [ga_area[:, 1024 + 384 * b:1408 + 384 * b] for b in range(2)]

        xsT = [h_area[:, 1024 * b:1024 * b + 1024].rearrange("p (k n) -> p k n", k=KD) for b in range(2)]
        act_T = qk_area[:, 0:512]
        ys = [qk_area[:, 512 + 512 * h:1024 + 512 * h] for h in range(2)]
        sig = qk_area[:, 1536:2048]
        glu = v_area[:, 0:512]
        lin = v_area[:, 512:1024]
        swi = conv_area[:, 0:512]
        act_sb = conv_area[:, 512:1024]
        conv_t = ga_area[:, 1792:2048]
        back = [conv_area[:, 1024 + 256 * b:1280 + 256 * b] for b in range(2)]
        pick = o_area[:, 0:256].rearrange("p (t s) -> p t s", t=NT)
        pickg = o_area[:, 256:512].rearrange("p (t s) -> p t s", t=NT)
        bsel = [o_area[:, 512 + 128 * b:640 + 128 * b] for b in range(2)]
        bias_gu = ga_area[:, :]
        bias_down = gc_area[0:E, 0:D]
        square = conv_area[:, 0:D]

        ident = sb("ident", [P, P])
        causal = sb("causal", [P, 2 * P])
        upto = sb("upto", [P, P])
        below = sb("below", [P, P])
        ones = sb("ones", [P, P])
        iota_i = sb("iota_i", [P, 64], I32)
        iota_f = sb("iota_f", [P, 64])
        slot_f = sb("slot_f", [P, CAP])
        part_i = sb("part_i", [P, 1], I32)
        part_f = sb("part_f", [P, 1])
        w_fl = sb("w_fl", [P, KD, HEADS])
        w_rt = sb("w_rt", [P, KD, E])
        taps = sb("taps", [P, 3, 4])
        bf_b = sb("bf_b", [P, HEADS])
        br_b = sb("br_b", [P, E])
        ss = sb("ss", [P, 3, NT])
        rstd = sb("rstd", [P, 3, NT])
        fz = sb("fz", [P, NT, HEADS])
        fa = sb("fa", [P, NT, HEADS])
        logf = sb("logf", [P, NT, HEADS])
        c_q = sb("c_q", [P, NT, HEADS])
        neg_c = sb("neg_c", [HEADS, SEQ])
        negmax = sb("negmax", [P, NT])
        psum_row = sb("psum_row", [P, NT])
        prec = sb("prec", [P, NT])
        table = conv_area[:, 1536:1536 + NT * 2 * TCOLS].rearrange("p (t c n) -> p t c n", t=NT, c=2)
        eq4 = v_area[:, 0:256].rearrange("p (t k e) -> p t k e", t=NT, k=TOPK)
        eg4 = v_area[:, 256:512].rearrange("p (t k e) -> p t k e", t=NT, k=TOPK)
        routeT = v_area[0:E, 512:1024].rearrange("p (c n) -> p c n", c=2)
        logits = qk_area[:, 0:NT * E].rearrange("p (t e) -> p t e", t=NT)
        route = qk_area[:, 64:64 + 3 * NT * E].rearrange("p (t c e) -> p t c e", t=NT, c=3)
        top8 = sb("top8", [P, NT, 8])
        idx8 = sb("idx8", [P, NT, 8], U32)
        idxf = sb("idxf", [P, NT, TOPK])
        topn = sb("topn", [P, NT])
        gexp = sb("gexp", [P, NT, TOPK])
        gsum = sb("gsum", [P, NT])
        gate4 = sb("gate4", [P, NT, TOPK])
        tasks = sb("tasks", [P, TCOLS])
        tstart = sb("tstart", [P, XCOLS])
        xneed = sb("xneed", [E, XROUNDS])
        xcount = sb("xcount", [E, 1])
        xbase = sb("xbase", [E, 1])
        xend = sb("xend", [E, 1])
        xge = qk_area[0:E, 512:512+XCOLS]
        xlt = qk_area[0:E, 576:576+XCOLS]
        xst = qk_area[0:E, 640:640+XCOLS]
        past = qk_area[:, 704:704 + XCOLS]
        xtot = sb("xtot", [P, 1])
        bodyn = sb("bodyn", [1, XBODIES])
        plan_i = sb("plan_i", [1, XCOLS + 1], I32)
        col_now = sb("col_now", [P, NT, 2, 2])

        slot_loaded = [sem(f"slot_loaded{s}") for s in range(NSLOT)]
        slot_freed = sem("slot_freed")
        x_loaded = sem("x_loaded")
        gmix_loaded = sem("gmix_loaded")
        gffn_loaded = sem("gffn_loaded")
        small_loaded = sem("small_loaded")
        gfinal_loaded = sem("gfinal_loaded")
        biases_loaded = sem("biases_loaded")
        consts_made = sem("consts_made")
        pool_step = sem("pool_step")
        dve_step = sem("dve_step")
        squares_summed = sem("squares_summed")
        meansq_ready = sem("meansq_ready")
        root_ready = sem("root_ready")
        h_ready = sem("h_ready")
        h_turned = sem("h_turned")
        hT_by_scalar = sem("hT_by_scalar")
        hT_by_vector = sem("hT_by_vector")
        tile_ready = sem("tile_ready")
        tile_read_s = sem("tile_read_s")
        tile_read_v = sem("tile_read_v")
        forget_ready = sem("forget_ready")
        forget_abs = sem("forget_abs")
        forget_exp = sem("forget_exp")
        forget_exp1 = sem("forget_exp1")
        forget_ln = sem("forget_ln")
        logf_ready = sem("logf_ready")
        cumsum_ready = sem("cumsum_ready")
        cumsum_read = sem("cumsum_read")
        scores_ready = sem("scores_ready")
        scores_read = sem("scores_read")
        negmax_ready = sem("negmax_ready")
        exp_ready = sem("exp_ready")
        probs_ready = sem("probs_ready")
        probs_turned = sem("probs_turned")
        probsT_ready = sem("probsT_ready")
        pv_done = sem("pv_done")
        oT_ready = sem("oT_ready")
        merged = sem("merged")
        mixer_out = sem("mixer_out")
        logits_ready = sem("logits_ready")
        top_ready = sem("top_ready")
        gexp_ready = sem("gexp_ready")
        chosen_ready = sem("chosen_ready")
        rank_ready = sem("rank_ready")
        route_ready = sem("route_ready")
        route_turned = sem("route_turned")
        routeT_ready = sem("routeT_ready")
        xcount_ready = sem("xcount_ready")
        xbase_ready = sem("xbase_ready")
        xtasks_ready = sem("xtasks_ready")
        plan_ready = sem("plan_ready")
        plan_stored = sem("plan_stored")
        table_ready = sem("table_ready")
        cleared = sem("cleared")
        pick_step = sem("pick_step")
        pick_ready = sem("pick_ready")
        gathered = sem("gathered")
        xsT_ready = sem("xsT_ready")
        back_turned = sem("back_turned")
        back_ready = sem("back_ready")
        gu_ready = sem("gu_ready")
        glu_clamped = sem("glu_clamped")
        gu_read = sem("gu_read")
        sigmoid_ready = sem("sigmoid_ready")
        swi_ready = sem("swi_ready")
        act_ready = sem("act_ready")
        act_turned = sem("act_turned")
        actT_ready = sem("actT_ready")
        down_ready = sem("down_ready")
        ys_ready = sem("ys_ready")
        combined = sem("combined")
        moe_ready = sem("moe_ready")
        final_ready = sem("final_ready")
        out_stored = sem("out_stored")

        w_in_k = w_in.rearrange("(k p) n -> p k n", p=P)
        proj = [w.rearrange("(k p) n -> p k n", p=P) for w in (w_conv_o, w_attn_o, w_out)]
        gu_k = w_gate_up.rearrange("e (k p) n -> e p k n", p=P)
        dn_k = w_down.rearrange("e (k p) n -> e p k n", p=P)

        def mixer_source(u):
            if u < 2 * GROUPS:
                c = GROUP_COL[u // 2]
                return w_in_k[:, 4 * (u % 2):4 * (u % 2) + 4, c:c + 512]
            u -= 2 * GROUPS
            which, half = (0, u) if u < 2 else (1, u - 2) if u < 4 else (2, u - 4)
            return proj[which][:, 2 * half:2 * half + 2, :]

        def mixer_freed(u):
            if u < 2 * GROUPS:
                i = len(TILES) - 1
                while GROUP_OF.get(TILES[i][0], 99) + (TILES[i][1] // 4 if TILES[i][0] != "v" else 0) != u // 2:
                    i -= 1
                return i + 1
            u -= 2 * GROUPS
            return TILES.index(("yc", KD - 1) if u < 2 else ("ya", KD - 1) if u < 4 else ("x", 2 * NT - 1)) + 1

        def in_slot(u, k):
            return ring[:, u % NSLOT, :].rearrange("p (k n) -> p k n", k=k)

        block = ctx.enter_context(nc.Block())

        @block.sync
        def _(sp):
            for t in range(NT):
                sp.dma_start(x_res[:, t, :], x[0, P * t:P * t + P, :]).then_inc(x_loaded, 16)
            for u in range(MIXER_USES):
                if u >= NSLOT:
                    sp.wait_ge(tile_ready, mixer_freed(u - NSLOT))
                sp.dma_start(in_slot(u, 4 if u < 2 * GROUPS else 2), mixer_source(u)).then_inc(slot_loaded[u % NSLOT], 16)

            def wait_for_slot(it, j, i):
                before = TASK_USES * j + i - NSLOT
                task, use = j + (before - TASK_USES * j) // TASK_USES, before % TASK_USES
                if isinstance(it, int) and TASK_USES * TPB * it + before < 0:
                    sp.wait_ge(tile_ready, mixer_freed(MIXER_USES + before))
                elif use in (7, TASK_USES - 1):
                    sp.wait_ge(gu_ready if use == 7 else down_ready, it * TPB + (task + 1))
                else:
                    sp.wait_ge(slot_freed, it * (TPB * FREED) + (FREED * task + use + (use < 7)))

            def stream_task(e, it, j):
                for i in range(TASK_USES):
                    u = MIXER_USES + TASK_USES * j + i
                    wait_for_slot(it, j, i)
                    if i < 8:
                        sp.dma_start(ring[:, u % NSLOT, :], gu_k[e, :, i, :]).then_inc(slot_loaded[u % NSLOT], 16)
                    else:
                        sp.dma_start(in_slot(u, 2), dn_k[e, :, 2 * (i - 8):2 * (i - 8) + 2, :])\
                          .then_inc(slot_loaded[u % NSLOT], 16)

            for j in range(TPB):
                stream_task(j, 0, j)
            with sp.Fori(1, E // TPB) as it:
                for j in range(TPB):
                    stream_task(it * TPB + j, it, j)
            sp.wait_ge(plan_ready, 1)
            bodies = sp.value_load(plan_i[0:1, XCOLS:XCOLS + 1], min_val=0, max_val=XBODIES)
            with sp.If(bodies > 0):
                with sp.Fori(0, bodies) as xt:
                    for j in range(TPB):
                        e = sp.value_load(plan_i[0:1, bass.ds(xt * TPB + j, 1)], min_val=0, max_val=E - 1)
                        stream_task(e, xt + E // TPB, j)
            sp.wait_ge(final_ready, 2)
            for t in range(NT):
                sp.dma_start(out[0, P * t:P * t + P, :], h_tok[:, t, :]).then_inc(out_stored, 16)
            sp.wait_ge(out_stored, 16 * NT)

        @block.gpsimd
        def _(pool):
            n = [0]

            def step(ins):
                n[0] += 1
                ins.then_inc(pool_step, 1)
                pool.wait_ge(pool_step, n[0])

            def all_of(tensor, value):
                step(pool.memset(tensor, value))

            def select(m, op, fill, base, step_x, mult, width=P):
                step(pool.affine_select(out=m, in_=m, compare_op=op, fill=fill, base=base,
                                        pattern=[[step_x, width]], channel_multiplier=mult))

            all_of(ident[:, :], 0.0)
            select(ident[:, :], ALU.not_equal, 1.0, 0, -1, 1)
            pool.nop().then_inc(consts_made, 1)
            all_of(ones[:, :], 1.0)
            all_of(upto[:, :], 1.0)
            select(upto[:, :], ALU.is_ge, 0.0, 0, 1, -1)
            all_of(below[:, :], 1.0)
            select(below[:, :], ALU.is_gt, 0.0, 0, 1, -1)
            all_of(causal[:, :], 0.0)
            select(causal[:, P:2 * P], ALU.is_ge, MASKED, 0, -1, 1)
            step(pool.iota(iota_i[:, :], pattern=[[1, 64]], base=0, channel_multiplier=0))
            step(pool.iota(part_i[:, :], pattern=[[0, 1]], base=0, channel_multiplier=1))
            step(pool.tensor_copy(iota_f[:, :], iota_i[:, :]))
            step(pool.tensor_copy(part_f[:, :], part_i[:, :]))
            step(pool.tensor_copy(slot_f[:, :], iota_f[:, 0:CAP]))
            if USED < CAP:
                step(pool.memset(slot_f[:, USED:CAP], 8192.0))
            for m in range(4):
                step(pool.memset(u_pad[:, m, 0:2], 0.0))
            step(pool.memset(tasks[:, :], 0.0))
            step(pool.tensor_copy(tasks[:, 0:E], ident[:, 0:E]))
            pool.nop().then_inc(consts_made, 1)
            pool.wait_ge(h_ready, NT)
            pool.dma_start(gain[:, 0, :], g_final.rearrange("(a n) -> a n", a=1).broadcast_to([P, D]))\
                .then_inc(gfinal_loaded, 16)
            pool.wait_ge(merged, KD)
            step(pool.memset(bias_gu, 0.0))
            pool.dma_start(bias_gu[0:E, :], b_gate_up).then_inc(biases_loaded, 16)
            pool.wait_ge(mixer_out, NT)
            pool.dma_start(bias_down, b_down).then_inc(biases_loaded, 16)

        @block.scalar
        def _(act):
            def spread(vector, n):
                return vector.rearrange("(a n) -> a n", a=1).broadcast_to([P, n])

            act.dma_start(gain[:, 0, :], spread(g_mix, D)).then_inc(gmix_loaded, 16)
            act.dma_start(w_fl[:, :, :], w_in_k[:, :, FORGET_COL:FORGET_COL + HEADS]).then_inc(small_loaded, 16)
            act.dma_start(bf_b[:, :], spread(b_f, HEADS)).then_inc(small_loaded, 16)
            act.dma_start(taps[:, :, :], conv_w).then_inc(small_loaded, 16)
            act.dma_start(w_rt[:, :, :], w_router.rearrange("(k p) n -> p k n", p=P)).then_inc(small_loaded, 16)
            act.dma_start(br_b[:, :], spread(b_router, E)).then_inc(small_loaded, 16)
            act.dma_start(gain[:, 1, :], spread(g_ffn, D)).then_inc(gffn_loaded, 16)

            def norm(which):
                for t in range(NT):
                    if which == 0:
                        act.wait_ge(x_loaded, 16 * NT)
                    elif which == 1:
                        act.wait_ge(mixer_out, NT)
                    else:
                        act.wait_ge(moe_ready, NT)
                    if t:
                        act.wait_ge(squares_summed, NT * which + t)
                    act.activation(square, x_res[:, t, :], ACT.Square, accum_out=ss[:, which, t:t + 1])\
                       .then_inc(squares_summed, 1)
                act.wait_ge(meansq_ready, which + 1)
                act.activation(rstd[:, which, :], rstd[:, which, :], ACT.Sqrt).then_inc(root_ready, 1)

            def copy_hT(round_, i):
                act.wait_ge(h_turned, 4 * round_ + i + 1)
                t, kk = i // 2, i % 2
                act.copy(hT[:, 4 * kk:4 * kk + 4, P * t:P * t + P],
                         ps[2 + i][:, :].rearrange("p (k n) -> p k n", k=4)).then_inc(hT_by_scalar, 1)

            def tile(i):
                kind, m = TILES[i]
                act.wait_ge(tile_ready, i + 1)
                src = ps[i % 2][:, 0:SEQ]
                if kind == "k":
                    ins = act.copy(kT[:, m, :], src)
                elif kind == "v":
                    ins = act.copy(v_tok[:, m, :], ps[i % 2][:, :])
                elif kind == "cc":
                    ins = act.copy(cc[:, m, :], src)
                elif kind == "gc":
                    ins = act.activation(gate_c[:, m, :], src, ACT.Sigmoid)
                else:
                    ins = act.activation(gate_a[:, m, :], src, ACT.Sigmoid)
                ins.then_inc(tile_read_s, 1)

            def copy_probs(h):
                act.wait_ge(probs_turned, h + 1)
                if h >= 2:
                    act.wait_ge(pv_done, h - 1)
                act.copy(pT_sb[h % 2], ps[4 + h % 2][:, 0:3 * P]).then_inc(probsT_ready, 1)

            norm(0)
            for i in (0, 2):
                copy_hT(0, i)
            first = len(QK_TILES)
            for i in range(4, first):
                tile(i)
            act.wait_ge(forget_abs, 1)
            act.activation(fa[:, :, :], fa[:, :, :], ACT.Exp, scale=-1.0).then_inc(forget_exp, 1)
            act.wait_ge(forget_exp1, 1)
            act.activation(fa[:, :, :], fa[:, :, :], ACT.Ln).then_inc(forget_ln, 1)
            for t in range(NT):
                tile(first + t)
            first += NT
            for s in range(len(CONV_TILES)):
                if TILES[first + s][0] in BY_SCALAR:
                    tile(first + s)
                if s < HEADS:
                    for t in range(NT):
                        w = P * (t + 1)
                        act.wait_ge(negmax_ready, NT * s + t + 1)
                        if s >= 1:
                            act.wait_ge(probs_turned, s)
                        act.activation(p_sb[t][:, 0:w], s_sb[t][:, 0:w], ACT.Exp, bias=negmax[:, t:t + 1],
                                       accum_out=psum_row[:, t:t + 1]).then_inc(exp_ready, 1)
                if 1 <= s <= HEADS:
                    copy_probs(s - 1)
            first += len(CONV_TILES)
            for i in range(len(GATE_TILES)):
                if i == KD:
                    act.wait_ge(pv_done, HEADS)
                    act.wait_ge(tile_read_v, tiles_read(TILES.index(("cb", 3)), False))
                tile(first + i)
            norm(1)
            for i in (0, 2):
                copy_hT(1, i)
            for t in range(NT):
                act.wait_ge(top_ready, t + 1)
                act.activation(gexp[:, t, :], top8[:, t, 0:TOPK], ACT.Exp, bias=topn[:, t:t + 1],
                               accum_out=gsum[:, t:t + 1]).then_inc(gexp_ready, 1)

            def copy_gathered(pair, parity, half):
                act.wait_ge(gathered, pair * 2 + half + 1)
                act.copy(xsT[parity][:, 4 * half:4 * half + 4, :],
                         ps[6][:, :].rearrange("p (k n) -> p k n", k=4)).then_inc(xsT_ready, 1)

            def copy_back(pair, parity):
                act.wait_ge(back_turned, pair + 1)
                act.copy(back[parity], ps[6][:, 0:SEQ]).then_inc(back_ready, 1)

            def task(n, pair, parity, b):
                act.wait_ge(glu_clamped, n + 1)
                act.activation(sig, glu, ACT.Sigmoid, scale=ALPHA).then_inc(sigmoid_ready, 1)
                copy_gathered(pair + 1, 1 - parity, b)
                act.wait_ge(act_turned, n + 1)
                act.copy(act_T, ps[7][:, :]).then_inc(actT_ready, 1)
                act.wait_ge(down_ready, n + 1)
                act.copy(ys[0][64 * b:64 * b + 64, :], ps[7][0:64, :]).then_inc(ys_ready, 1)
                act.copy(ys[1][64 * b:64 * b + 64, :], ps[7][64:128, :]).then_inc(ys_ready, 1)
                if b == 0:
                    copy_back(pair + 1, 1 - parity)

            def body(it):
                for j in range(TPB):
                    task(it * TPB + j, it * (TPB // 2) + j // 2, j // 2, j % 2)

            act.wait_ge(logits_ready, 1)
            for half in range(2):
                copy_gathered(0, 0, half)
            copy_back(0, 0)
            with act.Fori(0, E // TPB) as it:
                body(it)
            act.wait_ge(plan_ready, 1)
            bodies = act.value_load(plan_i[0:1, XCOLS:XCOLS + 1], min_val=0, max_val=XBODIES)
            with act.If(bodies > 0):
                with act.Fori(0, bodies) as xt:
                    body(xt + E // TPB)
            norm(2)

        @block.vector
        def _(dve):
            n = [0]

            def step(ins):
                n[0] += 1
                ins.then_inc(dve_step, 1)
                dve.wait_ge(dve_step, n[0])

            def norm(which, g, g_loaded, dst):
                dve.wait_ge(squares_summed, NT * (which + 1))
                dve.tensor_scalar(rstd[:, which, :], ss[:, which, :], 1.0 / D, EPS, ALU.mult, ALU.add)\
                   .then_inc(meansq_ready, 1)
                dve.wait_ge(root_ready, which + 1)
                step(dve.reciprocal(rstd[:, which, :], rstd[:, which, :]))
                dve.wait_ge(g_loaded, 16)
                for t in range(NT):
                    ins = dve.scalar_tensor_tensor(out=dst[:, t, :], in0=x_res[:, t, :], scalar=rstd[:, which, t:t + 1],
                                                   in1=gain[:, g, :], op0=ALU.mult, op1=ALU.mult)
                    ins.then_inc(final_ready if which == 2 else h_ready, 1)

            def copy_hT(round_, i):
                dve.wait_ge(h_turned, 4 * round_ + i + 1)
                t, kk = i // 2, i % 2
                dve.tensor_copy(hT[:, 4 * kk:4 * kk + 4, P * t:P * t + P],
                                ps[2 + i][:, :].rearrange("p (k n) -> p k n", k=4)).then_inc(hT_by_vector, 1)

            def tile(i):
                kind, m = TILES[i]
                if kind == "cb":
                    dve.wait_ge(tile_read_v, tiles_read(i - 1, False))
                    for j in range(3):
                        if j == 0:
                            step(dve.tensor_scalar(conv_t[:, :], u_pad[:, m, 0:SEQ], taps[:, 0, m:m + 1], None, ALU.mult))
                        else:
                            step(dve.scalar_tensor_tensor(out=conv_t[:, :], in0=u_pad[:, m, j:j + SEQ],
                                                          scalar=taps[:, j, m:m + 1], in1=conv_t[:, :],
                                                          op0=ALU.mult, op1=ALU.add))
                dve.wait_ge(tile_ready, i + 1)
                src = ps[i % 2][:, 0:SEQ]
                if kind == "q":
                    ins = dve.tensor_scalar(qT[:, m, :], src, HD ** -0.5, None, ALU.mult)
                elif kind == "cx":
                    dve.wait_ge(tile_read_s, tiles_read(TILES.index(("cc", m)), True))
                    ins = dve.tensor_tensor(u_pad[:, m, 2:2 + SEQ], src, cc[:, m, :], ALU.mult)
                elif kind == "cb":
                    ins = dve.tensor_tensor(cc[:, m, :], src, conv_t[:, :], ALU.mult)
                elif kind == "yc":
                    dve.wait_ge(tile_read_s, tiles_read(TILES.index(("gc", m)), True))
                    ins = dve.tensor_tensor(gate_c[:, m, :], src, gate_c[:, m, :], ALU.mult)
                elif kind == "ya":
                    dve.wait_ge(tile_read_s, tiles_read(TILES.index(("ga", m)), True))
                    ins = dve.tensor_tensor(gate_a[:, m, :], src, gate_a[:, m, :], ALU.mult)
                else:
                    t, half = m // 2, m % 2
                    xs = x_res[:, t, 512 * half:512 * half + 512]
                    ins = dve.tensor_tensor(xs, ps[i % 2][:, :], xs, ALU.add)
                ins.then_inc(tile_read_v, 1)
                if kind in ("cx", "yc"):
                    dve.wait_ge(tile_read_v, tiles_read(i, False))
                if kind == "ya":
                    dve.wait_ge(tile_read_v, tiles_read(i, False))
                    dve.tensor_tensor(gate_c[:, m, :], gate_c[:, m, :], gate_a[:, m, :], ALU.add).then_inc(merged, 1)
                if kind == "x" and half == 1:
                    dve.wait_ge(tile_read_v, tiles_read(i, False))
                    dve.engine_nop().then_inc(mixer_out, 1)

            norm(0, 0, gmix_loaded, h_tok)
            for i in (1, 3):
                copy_hT(0, i)
            for i in range(4):
                tile(i)
            dve.wait_ge(small_loaded, 16 * 5)
            dve.wait_ge(forget_ready, 1)
            step(dve.tensor_tensor(fz[:, :, :], ps[7][:, 0:NT * HEADS].rearrange("p (t h) -> p t h", t=NT),
                                   bf_b[:, :].rearrange("p (a h) -> p a h", a=1).broadcast_to([P, NT, HEADS]), ALU.add))
            step(dve.tensor_scalar(fa[:, :, :], fz[:, :, :], -1.0, None, ALU.mult))
            dve.tensor_tensor(fa[:, :, :], fa[:, :, :], fz[:, :, :], ALU.max).then_inc(forget_abs, 1)
            dve.wait_ge(forget_exp, 1)
            dve.tensor_scalar(fa[:, :, :], fa[:, :, :], 1.0, None, ALU.add).then_inc(forget_exp1, 1)
            dve.wait_ge(forget_ln, 1)
            dve.scalar_tensor_tensor(out=logf[:, :, :], in0=fz[:, :, :], scalar=0.0, in1=fa[:, :, :],
                                     op0=ALU.min, op1=ALU.subtract).then_inc(logf_ready, 1)
            dve.wait_ge(cumsum_ready, 1)
            dve.tensor_copy(c_q[:, :, :], ps[7][:, 16:32].rearrange("p (t h) -> p t h", t=NT)).then_inc(cumsum_read, 1)
            dve.tensor_scalar(neg_c[:, :], ps[7][0:HEADS, 64:64 + SEQ], -1.0, None, ALU.mult).then_inc(cumsum_read, 1)
            dve.wait_ge(cumsum_read, 2)
            first = len(QK_TILES) + NT
            dve.wait_ge(consts_made, 2)
            for s in range(len(CONV_TILES)):
                if TILES[first + s][0] not in BY_SCALAR:
                    tile(first + s)
                if s < HEADS:
                    for t in range(NT):
                        u, w = NT * s + t, P * (t + 1)
                        dve.wait_ge(scores_ready, u + 1)
                        dve.scalar_tensor_tensor(out=s_sb[t][:, 0:w], in0=ps[2 + t][:, 0:w], scalar=c_q[:, t, s:s + 1],
                                                 in1=causal[:, 2 * P - w:2 * P], op0=ALU.add, op1=ALU.add)\
                           .then_inc(scores_read, 1)
                        dve.wait_ge(scores_read, u + 1)
                        dve.tensor_reduce(negmax[:, t:t + 1], s_sb[t][:, 0:w], AX.X, ALU.max, negate=True)\
                           .then_inc(negmax_ready, 1)
                    for t in range(NT):
                        u, w = NT * s + t, P * (t + 1)
                        dve.wait_ge(exp_ready, u + 1)
                        step(dve.reciprocal(prec[:, t:t + 1], psum_row[:, t:t + 1]))
                        dve.tensor_scalar(p_sb[t][:, 0:w], p_sb[t][:, 0:w], prec[:, t:t + 1], None, ALU.mult)\
                           .then_inc(probs_ready, 1)
                if s >= 3 and (s - 3) % 2 == 0 and s - 3 < HEADS:
                    pair = (s - 3) // 2
                    dve.wait_ge(pv_done, 2 * pair + 2)
                    dve.tensor_copy(oT[:, pair, :], ps[6][:, 0:SEQ]).then_inc(oT_ready, 1)
            first += len(CONV_TILES) + len(GATE_TILES)
            for i in range(len(Y_TILES) + len(X_TILES)):
                if i == KD:
                    dve.wait_ge(tile_read_v, tiles_read(first + i - 1, False))
                tile(first + i)
            dve.wait_ge(tile_read_v, tiles_read(len(TILES) - 1, False))
            norm(1, 1, gffn_loaded, h_tok)
            for i in (1, 3):
                copy_hT(1, i)

            dve.wait_ge(logits_ready, 1)
            step(dve.tensor_tensor(logits[:, :, :], ps[7][:, 0:NT * E].rearrange("p (t e) -> p t e", t=NT),
                                   br_b[:, :].rearrange("p (a e) -> p a e", a=1).broadcast_to([P, NT, E]), ALU.add))
            for t in range(NT):
                step(dve.max(top8[:, t, :], logits[:, t, :]))
                dve.tensor_scalar(topn[:, t:t + 1], top8[:, t, 0:1], -1.0, None, ALU.mult).then_inc(top_ready, 1)
                step(dve.max_index(idx8[:, t, :], top8[:, t, :], logits[:, t, :]))
            step(dve.tensor_copy(idxf[:, :, :], idx8[:, :, 0:TOPK]))
            iota_e = iota_f[:, 0:E].rearrange("p (a e) -> p a e", a=1).broadcast_to([P, TOPK, E])
            for t in range(NT):
                step(dve.tensor_tensor(eq4[:, t, :, :], iota_e, idxf[:, t, :].rearrange("p (k a) -> p k a", a=1)
                                       .broadcast_to([P, TOPK, E]), ALU.is_equal))
                dve.tensor_reduce(route[:, t, 0, :], eq4[:, t, :, :].rearrange("p k e -> p e k"), AX.X, ALU.add)\
                   .then_inc(chosen_ready, 1)
                dve.wait_ge(gexp_ready, t + 1)
                step(dve.reciprocal(gsum[:, t:t + 1], gsum[:, t:t + 1]))
                step(dve.tensor_scalar(gate4[:, t, :], gexp[:, t, :], gsum[:, t:t + 1], None, ALU.mult))
                step(dve.tensor_tensor(eg4[:, t, :, :], eq4[:, t, :, :], gate4[:, t, :].rearrange("p (k a) -> p k a", a=1)
                                       .broadcast_to([P, TOPK, E]), ALU.mult))
                step(dve.tensor_reduce(route[:, t, 2, :], eg4[:, t, :, :].rearrange("p k e -> p e k"), AX.X, ALU.add))
            dve.wait_ge(rank_ready, 1)
            rank = ps[6][:, 0:NT * E].rearrange("p (t e) -> p t e", t=NT)
            step(dve.scalar_tensor_tensor(out=route[:, :, 1, :], in0=rank, scalar=1.0, in1=route[:, :, 0, :],
                                          op0=ALU.add, op1=ALU.mult))
            dve.tensor_scalar(route[:, :, 1, :], route[:, :, 1, :], -1.0, None, ALU.add).then_inc(route_ready, 1)
            counts = ps[6][0:E, 128:129]
            step(dve.tensor_scalar(xneed[:, :], iota_f[0:E, 1:1 + XROUNDS], float(USED), None, ALU.mult))
            step(dve.tensor_scalar(xneed[:, :], xneed[:, :], counts, None, ALU.is_lt))
            dve.tensor_reduce(xcount[:, :], xneed[:, :], AX.X, ALU.add).then_inc(xcount_ready, 1)
            dve.wait_ge(route_turned, 1)
            dve.tensor_copy(routeT[:, :, :], ps[7][0:E, :].rearrange("e (c n) -> e c n", c=2)).then_inc(routeT_ready, 1)
            dve.wait_ge(xbase_ready, 1)
            dve.tensor_copy(xtot[:, :], ps[6][:, 161:162]).then_inc(dve_step, 1)
            step(dve.tensor_copy(xbase[:, :], ps[6][0:E, 160:161]))
            n[0] += 1
            dve.wait_ge(dve_step, n[0])
            step(dve.tensor_tensor(xend[:, :], xbase[:, :], xcount[:, :], ALU.add))
            step(dve.tensor_scalar(xge[:, :], iota_f[0:E, 0:XCOLS], xbase[:, :], None, ALU.is_ge))
            step(dve.tensor_scalar(xlt[:, :], iota_f[0:E, 0:XCOLS], xend[:, :], None, ALU.is_lt))
            step(dve.tensor_tensor(tasks[0:E, E:TCOLS], xge[:, :], xlt[:, :], ALU.mult))
            step(dve.tensor_scalar(xst[:, :], iota_f[0:E, 0:XCOLS], xbase[:, :], 1.0, ALU.subtract, ALU.add))
            dve.scalar_tensor_tensor(out=xst[:, :], in0=xst[:, :], scalar=float(USED), in1=tasks[0:E, E:TCOLS],
                                     op0=ALU.mult, op1=ALU.mult).then_inc(xtasks_ready, 1)
            step(dve.tensor_scalar(past[:, :], iota_f[:, 0:XCOLS], xtot[:, :], 4096.0, ALU.is_ge, ALU.mult))
            step(dve.tensor_scalar(bodyn[:, :], iota_f[0:1, 0:XBODIES], float(TPB), None, ALU.mult))
            step(dve.tensor_scalar(bodyn[:, :], bodyn[:, :], xtot[0:1, :], None, ALU.is_lt))
            dve.wait_ge(plan_stored, 1)
            step(dve.tensor_tensor(tstart[:, :], ps[6][:, 192:192 + XCOLS], past[:, :], ALU.add))
            step(dve.tensor_reduce(past[0:1, 0:1], bodyn[:, :], AX.X, ALU.add))
            dve.tensor_copy(plan_i[:, XCOLS:XCOLS + 1], past[0:1, 0:1]).then_inc(dve_step, 1)
            n[0] += 1
            step(dve.tensor_copy(plan_i[:, 0:XCOLS], ps[6][0:1, 256:256 + XCOLS]))
            dve.engine_nop().then_inc(plan_ready, 1)
            tab = ps[7][:, 0:NT * 2 * TCOLS].rearrange("p (t c n) -> p t c n", t=NT, c=2)
            for t in range(NT):
                step(dve.tensor_copy(table[:, t, :, :], tab[:, t, :, :]))
                step(dve.tensor_tensor(table[:, t, 0, E:TCOLS], table[:, t, 0, E:TCOLS], tstart[:, :], ALU.subtract))
            dve.engine_nop().then_inc(table_ready, 1)

            for b in range(2):
                dve.memset(bsel[b], 0.0).then_inc(cleared, 1)
                dve.memset(ys[b], 0.0).then_inc(ys_ready, 1)
            dve.memset(back[1], 0.0).then_inc(cleared, 1)
            dve.wait_ge(cleared, 3)
            dve.engine_nop().then_inc(gu_read, 1)

            def make_pick(pair, parity):
                def own(ins, i):
                    ins.then_inc(pick_step, 1)
                    dve.wait_ge(pick_step, pair * (1 + 2 * NT) + i)
                own(dve.tensor_copy(col_now[:, :, :, :], table[:, :, :, bass.ds(pair * 2, 2)]), 1)
                slots = slot_f[:, :].rearrange("p (a s) -> p a s", a=1).broadcast_to([P, 2, CAP])
                for t in range(NT):
                    rank_b, gate_b = (col_now[:, t, c, :].rearrange("p (b a) -> p b a", a=1).broadcast_to([P, 2, CAP])
                                      for c in range(2))
                    own(dve.tensor_tensor(pick[:, t, :].rearrange("p (b s) -> p b s", b=2), slots, rank_b,
                                          ALU.is_equal), 2 + 2 * t)
                    own(dve.tensor_tensor(pickg[:, t, :].rearrange("p (b s) -> p b s", b=2),
                                          pick[:, t, :].rearrange("p (b s) -> p b s", b=2), gate_b, ALU.mult), 3 + 2 * t)
                dve.tensor_copy(bsel[parity][0:E, :].rearrange("p (b s) -> p b s", b=2),
                                tasks[0:E, bass.ds(pair * 2, 2)].rearrange("p (b a) -> p b a", a=1)
                                .broadcast_to([E, 2, CAP])).then_inc(pick_ready, 1)

            make_pick(0, 0)

            def task(n_task):
                dve.wait_ge(gu_ready, n_task + 1)
                dve.tensor_scalar(glu, ps[4][:, :], LIMIT, None, ALU.min).then_inc(glu_clamped, 1)
                dve.tensor_scalar(lin, ps[5][:, :], LIMIT, -LIMIT, ALU.min, ALU.max).then_inc(gu_read, 1)
                dve.wait_ge(sigmoid_ready, n_task + 1)
                dve.tensor_tensor(swi, glu, sig, ALU.mult).then_inc(swi_ready, 1)
                dve.wait_ge(swi_ready, n_task + 1)
                dve.wait_ge(gu_read, n_task + 2)
                dve.scalar_tensor_tensor(out=act_sb, in0=lin, scalar=1.0, in1=swi, op0=ALU.add, op1=ALU.mult)\
                   .then_inc(act_ready, 1)

            def body(it):
                for q in range(TPB // 2):
                    pair = it * (TPB // 2) + q
                    dve.wait_ge(gathered, pair * 2 + 2)
                    dve.wait_ge(back_turned, pair + 1)
                    make_pick(pair + 1, 1 - q)
                    for b in range(2):
                        task(it * TPB + 2 * q + b)

            with dve.Fori(0, E // TPB) as it:
                body(it)
            bodies = dve.value_load(plan_i[0:1, XCOLS:XCOLS + 1], min_val=0, max_val=XBODIES)
            with dve.If(bodies > 0):
                with dve.Fori(0, bodies) as xt:
                    body(xt + E // TPB)
            dve.wait_ge(combined, 1)
            for t in range(NT):
                for half in range(2):
                    xs = x_res[:, t, 512 * half:512 * half + 512]
                    ins = dve.tensor_tensor(xs, ps[2 * t + half][:, :], xs, ALU.add)
                ins.then_inc(moe_ready, 1)
            dve.wait_ge(moe_ready, NT)
            norm(2, 0, gfinal_loaded, h_tok)

        @block.tensor
        def _(pe):
            def turn_h(round_):
                for i in range(4):
                    t, kk = i // 2, i % 2
                    pe.wait_ge(h_ready, NT * round_ + t + 1)
                    for k in range(4):
                        c = P * (4 * kk + k)
                        ins = pe.transpose(ps[2 + i][:, P * k:P * k + P], h_tok[:, t, c:c + P], ident[:, :])
                    ins.then_inc(h_turned, 1)

            def slot_ready(u):
                pe.wait_ge(slot_loaded[u % NSLOT], 16 * (u // NSLOT + 1))

            def tile_bank(i):
                if i >= 2:
                    by_scalar = TILES[i - 2][0] in BY_SCALAR
                    pe.wait_ge(tile_read_s if by_scalar else tile_read_v, tiles_read(i - 2, by_scalar))
                return ps[i % 2]

            def in_tile(i):
                kind, m = TILES[i]
                g = GROUP_OF[kind] + m // 4
                bank = tile_bank(i)
                for k in range(KD):
                    u = 2 * g + k // 4
                    if m % 4 == 0 and k % 4 == 0:
                        slot_ready(u)
                    w = in_slot(u, 4)[:, k % 4, P * (m % 4):P * (m % 4) + P]
                    ins = pe.matmul(bank[:, 0:SEQ], w, hT[:, k, :], start=(k == 0), stop=(k == KD - 1))
                ins.then_inc(tile_ready, 1)

            def v_tile(i):
                t = TILES[i][1]
                bank = tile_bank(i)
                for k in range(KD):
                    u = 2 * GROUP_OF["v"] + k // 4
                    if k % 4 == 0:
                        slot_ready(u)
                    ins = pe.matmul(bank[:, :], hT[:, k, P * t:P * t + P], in_slot(u, 4)[:, k % 4, :],
                                    start=(k == 0), stop=(k == KD - 1))
                ins.then_inc(tile_ready, 1)

            def y_tile(i, use, src):
                m = TILES[i][1]
                bank = tile_bank(i)
                for k in range(4):
                    u = use + k // 2
                    if m == 0 and k % 2 == 0:
                        slot_ready(u)
                    ins = pe.matmul(bank[:, 0:SEQ], in_slot(u, 2)[:, k % 2, P * m:P * m + P], src[:, k, :],
                                    start=(k == 0), stop=(k == 3))
                ins.then_inc(tile_ready, 1)

            def x_tile(i):
                t, half = TILES[i][1] // 2, TILES[i][1] % 2
                bank = tile_bank(i)
                use = 2 * GROUPS + 4
                for k in range(KD):
                    u = use + k // 2
                    if t == 0 and half == 0 and k % 2 == 0:
                        slot_ready(u)
                    ins = pe.matmul(bank[:, :], gate_c[:, k, P * t:P * t + P],
                                    in_slot(u, 2)[:, k % 2, 512 * half:512 * half + 512],
                                    start=(k == 0), stop=(k == KD - 1))
                ins.then_inc(tile_ready, 1)

            def scores(h):
                m, lo = h // 2, HD * (h % 2)
                for t in range(NT):
                    u, w = NT * h + t, P * (t + 1)
                    if u >= NT:
                        pe.wait_ge(scores_read, u - NT + 1)
                    pe.matmul(ps[2 + t][:, 0:w], qT[lo:lo + HD, m, P * t:P * t + P], kT[lo:lo + HD, m, 0:w],
                              start=True, stop=False)
                    pe.matmul(ps[2 + t][:, 0:w], ident[0:HEADS, h:h + 1].broadcast_to([HEADS, P]), neg_c[:, 0:w],
                              start=False, stop=True).then_inc(scores_ready, 1)

            def turn_probs(h):
                pe.wait_ge(probs_ready, NT * h + NT)
                if h >= 2:
                    pe.wait_ge(probsT_ready, h - 1)
                bank = ps[4 + h % 2]
                pe.transpose(bank[:, 0:P], p_sb[0][:, 0:P], ident[:, :])
                pe.transpose(bank[:, P:2 * P], p_sb[1][:, 0:P], ident[:, :])
                pe.transpose(bank[:, 2 * P:3 * P], p_sb[1][:, P:2 * P], ident[:, :]).then_inc(probs_turned, 1)

            def values(h):
                pe.wait_ge(probsT_ready, h + 1)
                if h % 2 == 0 and h >= 2:
                    pe.wait_ge(oT_ready, h // 2)
                lo = HD * (h % 2)
                pe.matmul(ps[6][lo:lo + HD, 0:SEQ], v_tok[:, 0, HD * h:HD * h + HD], pT_sb[h % 2][:, 0:SEQ],
                          start=True, stop=False, skip_group_check=True)
                pe.matmul(ps[6][lo:lo + HD, P:SEQ], v_tok[:, 1, HD * h:HD * h + HD], pT_sb[h % 2][:, SEQ:3 * P],
                          start=False, stop=True, skip_group_check=True).then_inc(pv_done, 1)

            pe.wait_ge(consts_made, 1)
            turn_h(0)
            pe.wait_ge(hT_by_scalar, 2)
            pe.wait_ge(hT_by_vector, 2)
            first = len(QK_TILES)
            for i in range(first):
                in_tile(i)
            pe.wait_ge(small_loaded, 16 * 5)
            for t in range(NT):
                for k in range(KD):
                    ins = pe.matmul(ps[7][:, HEADS * t:HEADS * t + HEADS], hT[:, k, P * t:P * t + P], w_fl[:, k, :],
                                    start=(k == 0), stop=(k == KD - 1))
            ins.then_inc(forget_ready, 1)
            for t in range(NT):
                v_tile(first + t)
            first += NT
            pe.wait_ge(consts_made, 2)
            pe.wait_ge(logf_ready, 1)
            pe.matmul(ps[7][:, 16:24], upto[:, :], logf[:, 0, :], start=True, stop=True)
            pe.matmul(ps[7][:, 24:32], ones[:, :], logf[:, 0, :], start=True, stop=False)
            pe.matmul(ps[7][:, 24:32], upto[:, :], logf[:, 1, :], start=False, stop=True)
            pe.matmul(ps[7][0:HEADS, 64:192], logf[:, 0, :], upto[:, :], start=True, stop=True)
            pe.matmul(ps[7][0:HEADS, 192:320], logf[:, 0, :], ones[:, :], start=True, stop=False)
            pe.matmul(ps[7][0:HEADS, 192:320], logf[:, 1, :], upto[:, :], start=False, stop=True).then_inc(cumsum_ready, 1)
            pe.wait_ge(tile_read_v, 4)
            pe.wait_ge(tile_read_s, 4 + NT)
            for s in range(len(CONV_TILES)):
                in_tile(first + s)
                if s == 0:
                    pe.wait_ge(cumsum_read, 2)
                if s < HEADS:
                    scores(s)
                if 1 <= s <= HEADS:
                    turn_probs(s - 1)
                if 2 <= s <= HEADS + 1:
                    values(s - 2)
            first += len(CONV_TILES)
            for i in range(len(GATE_TILES)):
                in_tile(first + i)
            first += len(GATE_TILES)
            pe.wait_ge(tile_read_v, tiles_read(TILES.index(("cb", 3)), False))
            for i in range(KD):
                y_tile(first + i, 2 * GROUPS, cc)
            pe.wait_ge(oT_ready, HEADS // 2)
            for i in range(KD, 2 * KD):
                y_tile(first + i, 2 * GROUPS + 2, oT)
            pe.wait_ge(merged, KD)
            first += len(Y_TILES)
            for i in range(len(X_TILES)):
                x_tile(first + i)

            turn_h(1)
            pe.wait_ge(hT_by_scalar, 4)
            pe.wait_ge(hT_by_vector, 4)
            for t in range(NT):
                for k in range(KD):
                    ins = pe.matmul(ps[7][:, E * t:E * t + E], hT[:, k, P * t:P * t + P], w_rt[:, k, :],
                                    start=(k == 0), stop=(k == KD - 1))
            ins.then_inc(logits_ready, 1)
            pe.wait_ge(chosen_ready, NT)
            pe.matmul(ps[6][:, 0:E], below[:, :], route[:, 0, 0, :], start=True, stop=True)
            pe.matmul(ps[6][:, E:2 * E], ones[:, :], route[:, 0, 0, :], start=True, stop=False)
            pe.matmul(ps[6][:, E:2 * E], below[:, :], route[:, 1, 0, :], start=False, stop=True)
            for t in range(NT):
                ins = pe.matmul(ps[6][0:E, 128:129], route[:, t, 0, :], ones[:, 0:1], start=(t == 0), stop=(t == 1))
            ins.then_inc(rank_ready, 1)
            pe.wait_ge(route_ready, 1)
            for c in range(2):
                for t in range(NT):
                    ins = pe.transpose(ps[7][0:E, SEQ * c + P * t:SEQ * c + P * t + P], route[:, t, 1 + c, :], ident[:, :])
            ins.then_inc(route_turned, 1)
            pe.wait_ge(xcount_ready, 1)
            pe.matmul(ps[6][0:E, 160:161], below[0:E, 0:E], xcount[:, :], start=True, stop=True)
            pe.matmul(ps[6][:, 161:162], ones[0:E, :], xcount[:, :], start=True, stop=True).then_inc(xbase_ready, 1)
            pe.wait_ge(xtasks_ready, 1)
            pe.matmul(ps[6][:, 192:192 + XCOLS], ones[0:E, :], xst[:, :], start=True, stop=True)
            pe.wait_ge(routeT_ready, 1)
            for t in range(NT):
                for c in range(2):
                    at = (2 * t + c) * TCOLS
                    pe.matmul(ps[7][:, at:at + TCOLS], routeT[:, c, P * t:P * t + P], tasks[0:E, :], start=True, stop=True)
            pe.matmul(ps[6][0:1, 256:256 + XCOLS], part_f[0:E, :], tasks[0:E, E:TCOLS], start=True, stop=True)\
              .then_inc(plan_stored, 1)
            pe.wait_ge(biases_loaded, 32)
            for t in range(NT):
                for half in range(2):
                    pe.matmul(ps[2 * t + half][:, :], routeT[:, 1, P * t:P * t + P],
                              bias_down[:, 512 * half:512 * half + 512], start=True, stop=False, skip_group_check=True)

            def gather(pair, half):
                pe.wait_ge(pick_ready, pair + 1)
                for k in range(4):
                    c = P * (4 * half + k)
                    for t in range(NT):
                        ins = pe.matmul(ps[6][:, P * k:P * k + P], h_tok[:, t, c:c + P], pick[:, t, :],
                                        start=(t == 0), stop=(t == NT - 1))
                ins.then_inc(gathered, 1)

            def turn_back():
                for t in range(NT):
                    ins = pe.transpose(ps[6][:, P * t:P * t + P], pickg[:, t, :], ident[:, :])
                ins.then_inc(back_turned, 1)

            def combine(parity):
                for t in range(NT):
                    for half in range(2):
                        ins = pe.matmul(ps[2 * t + half][:, :], back[parity][:, P * t:P * t + P], ys[half],
                                        start=False, stop=False, skip_group_check=True)
                return ins

            def gate_up(it, j, b, parity):
                stationary = slice(CAP * b, CAP * b + CAP)
                for k in range(KD + 1):
                    u = MIXER_USES + TASK_USES * j + k
                    if k == 0:
                        lhsT, rows = bsel[parity][:, stationary], bias_gu
                    else:
                        u -= 1
                        pe.wait_ge(slot_loaded[u % NSLOT], it * (16 * TPB * TASK_USES // NSLOT) + 16 * (u // NSLOT + 1))
                        lhsT, rows = xsT[parity][:, k - 1, stationary], ring[:, u % NSLOT, :]
                    for g in range(4):
                        bank, lo = ps[4 + g // 2], 64 * (g % 2)
                        ins = pe.matmul(bank[lo:lo + 64, :], lhsT, rows[:, 512 * g:512 * g + 512],
                                        start=(k == 0), stop=(k == KD))
                    if k > 0:
                        ins.then_inc(slot_freed if k < KD else gu_ready, 1)

            def down(it, j):
                for k in range(KD):
                    u = MIXER_USES + TASK_USES * j + 8 + k // 2
                    if k % 2 == 0:
                        pe.wait_ge(slot_loaded[u % NSLOT], it * (16 * TPB * TASK_USES // NSLOT) + 16 * (u // NSLOT + 1))
                    lo = P * (k % 4) + 64 * (k // 4)
                    w = in_slot(u, 2)[:, k % 2, :]
                    for half in range(2):
                        ins = pe.matmul(ps[7][64 * half:64 * half + 64, :], act_T[:, lo:lo + 64],
                                        w[:, 512 * half:512 * half + 512], start=(k == 0), stop=(k == KD - 1))
                    if k % 2 == 1:
                        ins.then_inc(slot_freed if k < KD - 1 else down_ready, 1)

            def body(it):
                for j in range(TPB):
                    q, b = j // 2, j % 2
                    task, pair = it * TPB + j, it * (TPB // 2) + q
                    if b == 0:
                        pe.wait_ge(xsT_ready, pair * 2 + 2)
                    pe.wait_ge(gu_read, task + 1)
                    gate_up(it, j, b, q)
                    if b == 1:
                        pe.wait_ge(back_ready, pair + 2)
                    gather(pair + 1, b)
                    pe.wait_ge(ys_ready, task * 2 + 2)
                    if b == 0:
                        combine(1 - q)
                    pe.wait_ge(act_ready, task + 1)
                    for c in range(4):
                        ins = pe.transpose(ps[7][:, P * c:P * c + P], act_sb[:, P * c:P * c + P], ident[:, :])
                    ins.then_inc(act_turned, 1)
                    pe.wait_ge(actT_ready, task + 1)
                    down(it, j)
                    if b == 0:
                        pe.wait_ge(xsT_ready, pair * 2 + 3)
                        turn_back()

            pe.wait_ge(cleared, 3)
            pe.wait_ge(table_ready, 1)
            for half in range(2):
                if half:
                    pe.wait_ge(xsT_ready, 1)
                gather(0, half)
            pe.wait_ge(xsT_ready, 2)
            turn_back()
            pe.wait_ge(back_ready, 1)
            with pe.Fori(0, E // TPB) as it:
                body(it)
            pe.wait_ge(plan_ready, 1)
            bodies = pe.value_load(plan_i[0:1, XCOLS:XCOLS + 1], min_val=0, max_val=XBODIES)
            with pe.If(bodies > 0):
                with pe.Fori(0, bodies) as xt:
                    body(xt + E // TPB)
            pe.wait_ge(ys_ready, bodies * (2 * TPB) + (2 * E + 2))
            combine(1).then_inc(combined, 1)


_INS = ["x", "g_mix", "w_in", "conv_w", "b_f", "w_conv_o", "w_attn_o", "w_out", "g_ffn", "w_router", "b_router",
        "w_gate_up", "b_gate_up", "w_down", "b_down", "g_final"]


def kernel(**inputs):
    import numpy as _np
    import concourse.bacc as _bacc
    from concourse.bass_utils import run_bass_kernel_spmd as _run

    nc = _bacc.Bacc("TRN2", target_bir_lowering=False, num_devices=1)
    arrays, args = {}, []
    for name in _INS:
        a = _np.asarray(inputs[name])
        if name == "conv_w":
            a = a.reshape(3, CONV // P, P).transpose(2, 0, 1)
        a = _np.ascontiguousarray(a)
        arrays[f"in_{name}"] = a
        args.append(nc.dram_tensor(f"in_{name}", a.shape, mybir.dt.from_np(a.dtype), kind="ExternalInput").ap())
    args.append(nc.dram_tensor("out_0", (1, SEQ, D), F32, kind="ExternalOutput").ap())
    build(nc, *args)
    r = _run(nc, [arrays], core_ids=[0])
    return r.results[0]["out_0"]
```

```python
from contextlib import ExitStack

import concourse.bass as bass
from concourse import mybir

P = 128
D = 1024
SEQ = 256
NT = SEQ // P
KD = D // P
CONV = 512
HEADS = 8
HD = 64
ATT = HEADS * HD
E = 32
TOPK = 4
FF = 1024
LIMIT = 7.0
ALPHA = 1.702
EPS = 1e-5
NSLOT = 16
SLOT = 2048
CAP = 64
USED = 64
XROUNDS = SEQ // USED - 1
TPB = 4
BODIES = E // TPB
XTASKS = -(-(SEQ * TOPK // (USED + 1)) // TPB) * TPB
XCOLS = XTASKS + 2
TCOLS = E + XCOLS
XBODIES = XTASKS // TPB
W_IN_GROUPS = 10
MIXER_USES = 2 * W_IN_GROUPS + 2 + 2 + 4
TASK_USES = 12
FREED = TASK_USES - 2
MASKED = -1e30

F32 = mybir.dt.float32
F32R = mybir.dt.float32r
BF16 = mybir.dt.bfloat16
I32 = mybir.dt.int32
U32 = mybir.dt.uint32
ALU = mybir.AluOpType
ACT = mybir.ActivationFunctionType
AX = mybir.AxisListType

GROUPS = [("q", 0, 1536), ("k", 0, 2048), ("v", 0, 2560), ("cc", 0, 512), ("cx", 0, 1024), ("cb", 0, 0),
          ("gc", 0, 3080), ("gc", 1, 3592), ("ga", 0, 4104), ("ga", 1, 4616),
          ("yc", 0, 0), ("yc", 1, 512), ("ya", 0, 0), ("ya", 1, 512), ("x", 0, 0), ("x", 1, 512)]
FORGET_COL = 3072
TOKEN_MAJOR = ("v", "x")
BY_SCALAR = ("k", "v", "cc", "gc", "ga")
PROJ_USE = {"yc": 2 * W_IN_GROUPS, "ya": 2 * W_IN_GROUPS + 2, "x": 2 * W_IN_GROUPS + 4}
CHUNKS = [(g, k) for g, (kind, _, _) in enumerate(GROUPS) for k in range(4 if kind in ("yc", "ya") else KD)]
NCHUNK = len(CHUNKS)
NSPLIT = 3
HEAD_0, HEAD_STEP = 24, 3
CUMSUM_AT = 18


def group(kind, half=0):
    return [(k, h) for k, h, _ in GROUPS].index((kind, half))


def last_chunk(g):
    return max(c for c in range(NCHUNK) if CHUNKS[c][0] == g)


def use_of(c):
    g, k = CHUNKS[c]
    kind = GROUPS[g][0]
    return PROJ_USE[kind] + k // 2 if kind in PROJ_USE else 2 * g + k // 4


def chunks_done(u):
    return max(c for c in range(NCHUNK) if use_of(c) == u) + 1


def banks_read(g, b, by_scalar):
    return 2 * sum((k in BY_SCALAR) == by_scalar for k, _, _ in GROUPS[:g]) + b + 1


def build(nc, x, g_mix, w_in, conv_w, b_f, w_conv_o, w_attn_o, w_out, g_ffn, w_router, b_router,
          w_gate_up, b_gate_up, w_down, b_down, g_final, out):
    with ExitStack() as ctx:
        def sb(name, shape, dt=F32):
            return ctx.enter_context(nc.sbuf_tensor(name, shape, dt))

        def sem(name):
            return ctx.enter_context(nc.semaphore(name))

        ps = [ctx.enter_context(nc.psum_tensor(f"ps{i}", [P, 512], F32)) for i in range(8)]

        KB = 1024
        arena = sb("arena", [P, 201 * KB // 4])
        base = nc.sbuf_base - 201 * KB
        place, end = {}, base
        for name, size in (("ring", NSLOT * 8), ("x", 8), ("h", 8), ("w", 4), ("hT", 16), ("qk", 8), ("v", 4),
                           ("cc", 4), ("u", 5), ("gc", 8), ("ga", 8)):
            place[name] = end
            end += size * KB
        assert end - base == 201 * KB

        def at(name, where, off, shape, dt=F32):
            return nc.alloc_sbuf_tensor_at(name, shape, dt, offset=place[where] + off)

        ring = at("ring", "ring", 0, [P, NSLOT, SLOT])
        x_res = at("x_res", "x", 0, [P, NT, D])
        h_tok = at("h_tok", "h", 0, [P, NT, D])
        w_high = [at("w_high0", "w", 0, [P, 512], F32R)] + \
            [at(f"w_high{i}", "h", 4 * KB * (i - 1), [P, 512], F32R) for i in (1, 2)]
        w_low = [at("w_low0", "w", 2 * KB, [P, 512], F32R)] + \
            [at(f"w_low{i}", "h", 4 * KB * (i - 1) + 2 * KB, [P, 512], F32R) for i in (1, 2)]
        hT = [at(f"hT{i}", "hT", 8 * KB * i, [P, KD, SEQ], F32R) for i in range(2)]
        mT = [at(f"mT{i}", "hT", 8 * KB * i, [P, KD, SEQ], F32R) for i in range(2)]
        h2T = at("h2T", "hT", 0, [P, KD, SEQ])
        qT = at("qT", "qk", 0, [P, 4, SEQ])
        kT = at("kT", "qk", 4 * KB, [P, 4, SEQ])
        oT = [at(f"oT{i}", "qk", 4 * KB * i, [P, 4, SEQ], F32R) for i in range(2)]
        v_tok = at("v_tok", "v", 0, [P, NT, ATT])
        cc = at("cc", "cc", 0, [P, 4, SEQ])
        u_pad = at("u_pad", "u", 0, [P, 4, SEQ + 2])
        zT = [at("zT0", "cc", 0, [P, 4, SEQ], F32R), at("zT1", "u", 0, [P, 4, SEQ], F32R)]
        g_mix_b = at("g_mix_b", "gc", 0, [P, D])
        conv_s = at("conv_s", "gc", 0, [P, 4, SEQ])
        conv_t = at("conv_t", "gc", 4 * KB, [P, 4, SEQ])
        gate_c = at("gate_c", "gc", 0, [P, KD, SEQ])
        gate_a = at("gate_a", "ga", 0, [P, KD, SEQ])
        square0 = at("square0", "ga", 0, [P, 512])
        square1 = at("square1", "u", 0, [P, 512])
        square2 = at("square2", "cc", 0, [P, 512])
        s_sb = [at(f"s_sb{t}", "ga", KB * t, [P, SEQ]) for t in range(NT)]
        p_sb = [at(f"p_sb{t}", "ga", 2 * KB + KB * t, [P, SEQ]) for t in range(NT)]
        pT_sb = at("pT_sb", "ga", 4 * KB, [P, 3 * P])
        g_ffn_b = at("g_ffn_b", "v", 0, [P, D])
        w_rt = at("w_rt", "u", 3 * KB, [P, KD, E])

        logits = at("logits", "qk", 0, [P, NT, E])
        chosen = at("chosen", "qk", KB, [P, NT, E])
        eq4 = at("eq4", "qk", 2 * KB, [P, NT * TOPK, E])
        eg4 = at("eg4", "qk", 3 * KB, [P, NT * TOPK, E])

        xsT = [at(f"xsT{i}", "hT", 4 * KB * i, [P, KD, P]) for i in range(2)]
        pick = at("pick", "hT", 8 * KB, [P, NT, P])
        pickg = at("pickg", "hT", 9 * KB, [P, NT, P])
        bsel = [at(f"bsel{i}", "hT", 10 * KB + 512 * i, [P, P]) for i in range(2)]
        table = at("table", "hT", 11 * KB, [P, NT, 2, TCOLS])
        chosen_x = at("chosen_x", "hT", 14 * KB, [P, NT, E])
        act_T = at("act_T", "qk", 0, [P, 512])
        ys = [at(f"ys{h}", "qk", 2 * KB + 2 * KB * h, [P, 512]) for h in range(2)]
        sig = at("sig", "qk", 6 * KB, [P, 512])
        glu = at("glu", "v", 0, [P, 512])
        lin = at("lin", "v", 2 * KB, [P, 512])
        routeT = at("routeT", "v", 2 * KB, [E, 2, SEQ])
        xge = at("xge", "v", 0, [E, XCOLS])
        xlt = at("xlt", "v", 256, [E, XCOLS])
        xst = at("xst", "v", 512, [E, XCOLS])
        past = at("past", "v", 768, [P, XCOLS])
        swi = at("swi", "cc", 0, [P, 512])
        act_sb = at("act_sb", "cc", 2 * KB, [P, 512])
        back = [at(f"back{i}", "u", KB * i, [P, SEQ]) for i in range(2)]
        bias_gu = at("bias_gu", "ga", 0, [P, 2 * FF])
        bias_down = at("bias_down", "gc", 0, [E, D])
        g_final_b = at("g_final_b", "gc", 4 * KB, [P, D])

        ident = sb("ident", [P, P])
        causal = sb("causal", [P, 2 * P])
        upto = sb("upto", [P, P])
        below = sb("below", [P, P])
        ones = sb("ones", [P, P])
        iota_i = sb("iota_i", [P, 64], I32)
        iota_f = sb("iota_f", [P, 64])
        slot_f = sb("slot_f", [P, CAP]) if USED < CAP else iota_f
        part_i = sb("part_i", [P, 1], I32)
        part_f = sb("part_f", [P, 1])
        warm = sb("warm", [P, 8])
        w_fl = sb("w_fl", [P, KD, HEADS])
        fl_high = sb("fl_high", [P, KD, HEADS], F32R)
        fl_low = sb("fl_low", [P, KD, HEADS], F32R)
        taps = sb("taps", [P, 3, 4])
        bf_b = sb("bf_b", [P, HEADS])
        br_b = sb("br_b", [P, E])
        ss = sb("ss", [P, 3, NT, 2])
        rstd = sb("rstd", [P, 3, NT])
        fz = sb("fz", [P, NT, HEADS])
        fa = sb("fa", [P, NT, HEADS])
        logf = sb("logf", [P, NT, HEADS])
        c_q = sb("c_q", [P, NT, HEADS])
        neg_c = at("neg_c", "ga", 5 * KB + 512, [HEADS, SEQ])
        negmax = sb("negmax", [P, NT])
        psum_row = sb("psum_row", [P, NT])
        prec = sb("prec", [P, NT])
        top8 = sb("top8", [P, NT, 8])
        idx8 = sb("idx8", [P, NT, 8], U32)
        idxf = sb("idxf", [P, NT, TOPK])
        topn = sb("topn", [P, NT])
        gexp = sb("gexp", [P, NT, TOPK])
        gsum = sb("gsum", [P, NT])
        grec = sb("grec", [P, NT])
        gate4 = sb("gate4", [P, NT, TOPK])
        tasks = sb("tasks", [P, TCOLS])
        tstart = sb("tstart", [P, XCOLS])
        xneed = sb("xneed", [E, XROUNDS])
        xcount = sb("xcount", [E, 1])
        xbase = sb("xbase", [E, 1])
        xend = sb("xend", [E, 1])
        xtot = sb("xtot", [P, 1])
        bodyn = sb("bodyn", [1, XBODIES])
        plan_i = sb("plan_i", [1, XCOLS + 1], I32)
        col_now = sb("col_now", [P, NT, 2, 2])

        slot_loaded = [sem(f"slot_loaded{s}") for s in range(NSLOT)]
        x_loaded = [sem(f"x_loaded{t}") for t in range(NT)]
        low_ready = sem("low_ready")
        slot_freed = sem("slot_freed")
        plan_ready = sem("plan_ready")
        final_ready = sem("final_ready")
        out_stored = sem("out_stored")
        pool_step = sem("pool_step")
        warm_made = sem("warm_made")
        consts_made = sem("consts_made")
        small_loaded = sem("small_loaded")
        h_ready = sem("h_ready")
        bank_read_v = sem("bank_read_v")
        conv_ready = sem("conv_ready")
        pv_done = sem("pv_done")
        gffn_loaded = sem("gffn_loaded")
        chunk_used = sem("chunk_used")
        wrt_loaded = sem("wrt_loaded")
        merged_ready = sem("merged_ready")
        bgu_loaded = sem("bgu_loaded")
        mlow_ready = sem("mlow_ready")
        bdown_loaded = sem("bdown_loaded")
        gfinal_loaded = sem("gfinal_loaded")
        gmix_loaded = sem("gmix_loaded")
        squares_summed = sem("squares_summed")
        sumsq_ready = sem("sumsq_ready")
        root_ready = sem("root_ready")
        high_ready = sem("high_ready")
        bank_read_s = sem("bank_read_s")
        h_turned = sem("h_turned")
        hT_high = sem("hT_high")
        fl_high_ready = sem("fl_high_ready")
        zlow_ready = sem("zlow_ready")
        z_ready = sem("z_ready")
        zhigh_ready = sem("zhigh_ready")
        mhigh_ready = sem("mhigh_ready")
        forget_abs = sem("forget_abs")
        forget_exp = sem("forget_exp")
        forget_exp1 = sem("forget_exp1")
        forget_ln = sem("forget_ln")
        negmax_ready = sem("negmax_ready")
        probs_turned = sem("probs_turned")
        exp_ready = sem("exp_ready")
        probsT_ready = sem("probsT_ready")
        ohigh_ready = sem("ohigh_ready")
        h2T_by_scalar = sem("h2T_by_scalar")
        top_ready = sem("top_ready")
        gexp_ready = sem("gexp_ready")
        gathered = sem("gathered")
        xsT_ready = sem("xsT_ready")
        back_turned = sem("back_turned")
        back_ready = sem("back_ready")
        glu_clamped = sem("glu_clamped")
        sigmoid_ready = sem("sigmoid_ready")
        act_turned = sem("act_turned")
        actT_ready = sem("actT_ready")
        down_ready = sem("down_ready")
        ys_ready = sem("ys_ready")
        logits_ready = sem("logits_ready")
        moe_ready = sem("moe_ready")
        dve_step = sem("dve_step")
        hT_low = sem("hT_low")
        fl_low_ready = sem("fl_low_ready")
        forget_ready = sem("forget_ready")
        logf_ready = sem("logf_ready")
        cumsum_ready = sem("cumsum_ready")
        cumsum_read = sem("cumsum_read")
        scores_ready = sem("scores_ready")
        scores_read = sem("scores_read")
        probs_ready = sem("probs_ready")
        olow_ready = sem("olow_ready")
        h2T_by_vector = sem("h2T_by_vector")
        cleared = sem("cleared")
        index_ready = sem("index_ready")
        chosen_ready = sem("chosen_ready")
        rank_ready = sem("rank_ready")
        pick_step = sem("pick_step")
        pick_ready = sem("pick_ready")
        chosen_kept = sem("chosen_kept")
        gu_read = sem("gu_read")
        gu_ready = sem("gu_ready")
        swi_ready = sem("swi_ready")
        act_ready = sem("act_ready")
        counts_ready = sem("counts_ready")
        xcount_ready = sem("xcount_ready")
        route_turned = sem("route_turned")
        routeT_ready = sem("routeT_ready")
        xbase_ready = sem("xbase_ready")
        xtasks_ready = sem("xtasks_ready")
        plan_turned = sem("plan_turned")
        table_ready = sem("table_ready")
        combined = sem("combined")
        h2_ready = sem("h2_ready")

        w_in_k = w_in.rearrange("(k p) n -> p k n", p=P)
        proj = {"yc": w_conv_o.rearrange("(k p) n -> p k n", p=P), "ya": w_attn_o.rearrange("(k p) n -> p k n", p=P),
                "x": w_out.rearrange("(k p) n -> p k n", p=P)}
        gu_k = w_gate_up.rearrange("e (k p) n -> e p k n", p=P)
        dn_k = w_down.rearrange("e (k p) n -> e p k n", p=P)

        def in_slot(u, k):
            return ring[:, u % NSLOT, :].rearrange("p (k n) -> p k n", k=k)

        def mixer_source(u):
            c = [use_of(c) for c in range(NCHUNK)].index(u)
            g, k = CHUNKS[c]
            kind, _, col = GROUPS[g]
            if kind in PROJ_USE:
                return proj[kind][:, k:k + 2, :]
            return w_in_k[:, k:k + 4, col:col + 512]

        def chunk_in_ring(c):
            g, k = CHUNKS[c]
            kind, _, col = GROUPS[g]
            if kind in PROJ_USE:
                return in_slot(use_of(c), 2)[:, k % 2, col:col + 512]
            return in_slot(use_of(c), 4)[:, k % 4, :]

        def group_bank(g, b):
            return ps[2 * (g % 2) + b]

        block = ctx.enter_context(nc.Block())

        @block.sync
        def _(sp):
            for t in range(NT):
                sp.dma_start(x_res[:, t, :], x[0, P * t:P * t + P, :]).then_inc(x_loaded[t], 16)
            for u in range(MIXER_USES):
                if u >= NSLOT:
                    sp.wait_ge(low_ready, chunks_done(u - NSLOT))
                sp.dma_start(in_slot(u, 2 if u >= 2 * W_IN_GROUPS else 4), mixer_source(u)).then_inc(slot_loaded[u % NSLOT], 16)

            def wait_for_slot(it, j, i):
                before = TASK_USES * j + i - NSLOT
                task, use = j + (before - TASK_USES * j) // TASK_USES, before % TASK_USES
                if isinstance(it, int) and TASK_USES * TPB * it + before < 0:
                    sp.wait_ge(low_ready, chunks_done(MIXER_USES + before))
                elif use in (7, TASK_USES - 1):
                    sp.wait_ge(gu_ready if use == 7 else down_ready, it * TPB + (task + 1))
                else:
                    sp.wait_ge(slot_freed, it * (TPB * FREED) + (FREED * task + use + (use < 7)))

            def stream_task(e, it, j):
                for i in range(TASK_USES):
                    u = MIXER_USES + TASK_USES * j + i
                    wait_for_slot(it, j, i)
                    if i < 8:
                        sp.dma_start(ring[:, u % NSLOT, :], gu_k[e, :, i, :]).then_inc(slot_loaded[u % NSLOT], 16)
                    else:
                        sp.dma_start(in_slot(u, 2), dn_k[e, :, 2 * (i - 8):2 * (i - 8) + 2, :])\
                          .then_inc(slot_loaded[u % NSLOT], 16)

            for j in range(TPB):
                stream_task(j, 0, j)
            with sp.Fori(1, BODIES) as it:
                for j in range(TPB):
                    stream_task(it * TPB + j, it, j)
            sp.wait_ge(plan_ready, 1)
            bodies = sp.value_load(plan_i[0:1, XCOLS:XCOLS + 1], min_val=0, max_val=XBODIES)
            with sp.If(bodies > 0):
                with sp.Fori(0, bodies) as xt:
                    for j in range(TPB):
                        e = sp.value_load(plan_i[0:1, bass.ds(xt * TPB + j, 1)], min_val=0, max_val=E - 1)
                        stream_task(e, xt + BODIES, j)
            for t in range(NT):
                sp.wait_ge(final_ready, t + 1)
                sp.dma_start(out[0, P * t:P * t + P, :], h_tok[:, t, :]).then_inc(out_stored, 16)
            sp.wait_ge(out_stored, 16 * NT)

        @block.gpsimd
        def _(pool):
            n = [0]

            def step(ins):
                n[0] += 1
                ins.then_inc(pool_step, 1)
                pool.wait_ge(pool_step, n[0])

            def all_of(tensor, value):
                step(pool.memset(tensor, value))

            def select(m, op, fill, base, step_x, mult):
                step(pool.affine_select(out=m, in_=m, compare_op=op, fill=fill, base=base,
                                        pattern=[[step_x, P]], channel_multiplier=mult))

            all_of(warm[:, :], 1.0)
            pool.nop().then_inc(warm_made, 1)
            all_of(ident[:, :], 0.0)
            select(ident[:, :], ALU.not_equal, 1.0, 0, -1, 1)
            pool.nop().then_inc(consts_made, 1)
            all_of(ones[:, :], 1.0)
            all_of(upto[:, :], 1.0)
            select(upto[:, :], ALU.is_ge, 0.0, 0, 1, -1)
            all_of(below[:, :], 1.0)
            select(below[:, :], ALU.is_gt, 0.0, 0, 1, -1)
            all_of(causal[:, :], 0.0)
            select(causal[:, P:2 * P], ALU.is_ge, MASKED, 0, -1, 1)
            step(pool.iota(iota_i[:, :], pattern=[[1, 64]], base=0, channel_multiplier=0))
            step(pool.iota(part_i[:, :], pattern=[[0, 1]], base=0, channel_multiplier=1))
            step(pool.tensor_copy(iota_f[:, :], iota_i[:, :]))
            step(pool.tensor_copy(part_f[:, :], part_i[:, :]))
            if USED < CAP:
                step(pool.tensor_copy(slot_f[:, :], iota_f[:, 0:CAP]))
                step(pool.memset(slot_f[:, USED:CAP], 8192.0))
            for m in range(4):
                step(pool.memset(u_pad[:, m, 0:2], 0.0))
            step(pool.memset(tasks[:, :], 0.0))
            step(pool.tensor_copy(tasks[:, 0:E], ident[:, 0:E]))
            pool.nop().then_inc(consts_made, 1)
            pool.wait_ge(small_loaded, 16 * 4)
            pool.wait_ge(h_ready, NT)
            for m in range(4):
                if m % 2 == 0:
                    pool.wait_ge(bank_read_v, banks_read(group("cx"), m // 2, False))
                step(pool.tensor_scalar(conv_s[:, m, :], u_pad[:, m, 0:SEQ], taps[:, 0, m:m + 1], None, ALU.mult))
                for j in (1, 2):
                    step(pool.tensor_scalar(conv_t[:, m, :], u_pad[:, m, j:j + SEQ], taps[:, j, m:m + 1], None, ALU.mult))
                    step(pool.tensor_tensor(conv_s[:, m, :], conv_s[:, m, :], conv_t[:, m, :], ALU.add))
                pool.nop().then_inc(conv_ready, 1)
            pool.wait_ge(pv_done, HEADS)
            pool.dma_start(g_ffn_b[:, :], g_ffn.rearrange("(a n) -> a n", a=1).broadcast_to([P, D]))\
                .then_inc(gffn_loaded, 16)
            pool.wait_ge(chunk_used, last_chunk(group("yc", 1)) + 1)
            pool.dma_start(w_rt[:, :, :], w_router.rearrange("(k p) n -> p k n", p=P)).then_inc(wrt_loaded, 16)
            pool.wait_ge(merged_ready, 4)
            step(pool.memset(bias_gu[:, :], 0.0))
            pool.dma_start(bias_gu[0:E, :], b_gate_up).then_inc(bgu_loaded, 16)
            pool.wait_ge(mlow_ready, 4)
            pool.dma_start(bias_down[:, :], b_down).then_inc(bdown_loaded, 16)
            pool.dma_start(g_final_b[:, :], g_final.rearrange("(a n) -> a n", a=1).broadcast_to([P, D]))\
                .then_inc(gfinal_loaded, 16)

        @block.scalar
        def _(act):
            def spread(vector, n):
                return vector.rearrange("(a n) -> a n", a=1).broadcast_to([P, n])

            act.dma_start(g_mix_b[:, :], spread(g_mix, D)).then_inc(gmix_loaded, 16)
            act.dma_start(w_fl[:, :, :], w_in_k[:, :, FORGET_COL:FORGET_COL + HEADS]).then_inc(small_loaded, 16)
            act.dma_start(bf_b[:, :], spread(b_f, HEADS)).then_inc(small_loaded, 16)
            act.dma_start(taps[:, :, :], conv_w).then_inc(small_loaded, 16)
            act.dma_start(br_b[:, :], spread(b_router, E)).then_inc(small_loaded, 16)

            def load_table(func, i):
                if i == 0:
                    act.wait_ge(warm_made, 1)
                act.activation(warm[:, 1 + i:2 + i], warm[:, 0:1], func)

            def squares(which, t, half, scratch):
                done = 4 * which + (2 * t + half if which != 1 else 2 * half + t)
                if done:
                    act.wait_ge(squares_summed, done)
                act.activation(scratch[:, :], x_res[:, t, 512 * half:512 * half + 512], ACT.Square,
                               accum_out=ss[:, which, t, half:half + 1]).then_inc(squares_summed, 1)

            def root(which, t):
                act.wait_ge(sumsq_ready, NT * which + t + 1)
                act.activation(rstd[:, which, t:t + 1], rstd[:, which, t:t + 1], ACT.Sqrt, scale=1.0 / D)\
                   .then_inc(root_ready, 1)

            def high_part(c):
                if c == 0 or use_of(c) != use_of(c - 1):
                    u = use_of(c)
                    act.wait_ge(slot_loaded[u % NSLOT], 16 * (u // NSLOT + 1))
                if c >= NSPLIT:
                    act.wait_ge(chunk_used, c - NSPLIT + 1)
                act.copy(w_high[c % NSPLIT][:, :], chunk_in_ring(c)).then_inc(high_ready, 1)

            def read_bank(g, b):
                kind, half, _ = GROUPS[g]
                act.wait_ge(chunk_used, last_chunk(g) + 1)
                src = group_bank(g, b)[:, :]
                two = src.rearrange("p (m n) -> p m n", m=2)
                m = 4 * half + 2 * b
                if kind == "k":
                    ins = act.copy(kT[:, m:m + 2, :], two)
                elif kind == "v":
                    ins = act.copy(v_tok[:, b, :], src)
                elif kind == "cc":
                    ins = act.copy(cc[:, m:m + 2, :], two)
                elif kind == "gc":
                    ins = act.activation(gate_c[:, m:m + 2, :], two, ACT.Sigmoid)
                else:
                    ins = act.activation(gate_a[:, m:m + 2, :], two, ACT.Sigmoid)
                ins.then_inc(bank_read_s, 1)

            load_table(ACT.Sqrt, 0)
            for t in range(NT):
                act.wait_ge(x_loaded[t], 16)
                for half in range(2):
                    squares(0, t, half, square0)
                root(0, t)
            for i in range(4):
                act.wait_ge(h_turned, i + 1)
                t, kk = i // 2, i % 2
                act.copy(hT[0][:, 4 * kk:4 * kk + 4, P * t:P * t + P],
                         ps[4 + i][:, :].rearrange("p (k n) -> p k n", k=4)).then_inc(hT_high, 1)
            act.wait_ge(small_loaded, 16 * 4)
            act.copy(fl_high[:, :, :], w_fl[:, :, :]).then_inc(fl_high_ready, 1)
            load_table(ACT.Ln, 1)
            for c in range(NCHUNK + NSPLIT + 1):
                if c < NCHUNK:
                    high_part(c)
                for g, (kind, half, _) in enumerate(GROUPS):
                    if c != last_chunk(g) + NSPLIT:
                        continue
                    if kind in BY_SCALAR:
                        if kind == "gc" and half == 0:
                            act.wait_ge(zlow_ready, 2)
                            load_table(ACT.Sigmoid, 2)
                        if kind == "gc" and half == 1:
                            act.wait_ge(conv_ready, 4)
                        if kind == "ga" and half == 0:
                            act.wait_ge(pv_done, HEADS)
                        for b in range(2):
                            read_bank(g, b)
                    if kind == "cb":
                        for b in range(2):
                            act.wait_ge(z_ready, b + 1)
                            act.copy(zT[0][:, 2 * b:2 * b + 2, :], conv_s[:, 2 * b:2 * b + 2, :]).then_inc(zhigh_ready, 1)
                    if kind == "ya":
                        for b in range(2):
                            m = 4 * half + 2 * b
                            act.wait_ge(merged_ready, 2 * half + b + 1)
                            act.copy(mT[0][:, m:m + 2, :], gate_c[:, m:m + 2, :]).then_inc(mhigh_ready, 1)
                    if kind == "x":
                        for t in range(NT):
                            act.wait_ge(bank_read_v, banks_read(g, t, False))
                            squares(1, t, half, square1)
                if c == last_chunk(0) + NSPLIT:
                    act.wait_ge(forget_abs, 1)
                    act.activation(fa[:, :, :], fa[:, :, :], ACT.Exp, scale=-1.0).then_inc(forget_exp, 1)
                    act.wait_ge(forget_exp1, 1)
                    act.activation(fa[:, :, :], fa[:, :, :], ACT.Ln).then_inc(forget_ln, 1)
                h, off = divmod(c - HEAD_0 - NSPLIT, HEAD_STEP)
                if off == 0 and 0 <= h < HEADS:
                    for t in range(NT):
                        w = P * (t + 1)
                        act.wait_ge(negmax_ready, NT * h + t + 1)
                        if h >= 1:
                            act.wait_ge(probs_turned, h)
                        act.activation(p_sb[t][:, 0:w], s_sb[t][:, 0:w], ACT.Exp, bias=negmax[:, t:t + 1],
                                       accum_out=psum_row[:, t:t + 1]).then_inc(exp_ready, 1)
                h, off = divmod(c - HEAD_0 - NSPLIT - 4, HEAD_STEP)
                if off == 0 and 0 <= h < HEADS:
                    act.wait_ge(probs_turned, h + 1)
                    if h >= 1:
                        act.wait_ge(pv_done, h)
                    act.copy(pT_sb[:, :], ps[6][:, 0:3 * P]).then_inc(probsT_ready, 1)
                h, off = divmod(c - HEAD_0 - NSPLIT - 9, HEAD_STEP)
                if off == 0 and 0 <= h < HEADS and h % 2 == 1:
                    act.wait_ge(pv_done, h + 1)
                    act.copy(oT[0][:, h // 2, :], ps[7][:, 0:SEQ]).then_inc(ohigh_ready, 1)
            load_table(ACT.Sqrt, 3)
            for t in range(NT):
                root(1, t)
            load_table(ACT.Exp, 4)
            for i in (0, 2):
                act.wait_ge(h_turned, 4 + i + 1)
                t, kk = i // 2, i % 2
                act.copy(h2T[:, 4 * kk:4 * kk + 4, P * t:P * t + P],
                         ps[4 + i][:, :].rearrange("p (k n) -> p k n", k=4)).then_inc(h2T_by_scalar, 1)
            for t in range(NT):
                act.wait_ge(top_ready, t + 1)
                act.activation(gexp[:, t, :], top8[:, t, 0:TOPK], ACT.Exp, bias=topn[:, t:t + 1],
                               accum_out=gsum[:, t:t + 1]).then_inc(gexp_ready, 1)
            load_table(ACT.Sigmoid, 5)

            def copy_gathered(pair, parity, half):
                act.wait_ge(gathered, pair * 2 + half + 1)
                act.copy(xsT[parity][:, 4 * half:4 * half + 4, :],
                         ps[6][:, :].rearrange("p (k n) -> p k n", k=4)).then_inc(xsT_ready, 1)

            def copy_back(pair, parity):
                act.wait_ge(back_turned, pair + 1)
                act.copy(back[parity][:, :], ps[6][:, 0:SEQ]).then_inc(back_ready, 1)

            def task(n, pair, parity, b):
                act.wait_ge(glu_clamped, n + 1)
                act.activation(sig[:, :], glu[:, :], ACT.Sigmoid, scale=ALPHA).then_inc(sigmoid_ready, 1)
                copy_gathered(pair + 1, 1 - parity, b)
                act.wait_ge(act_turned, n + 1)
                act.copy(act_T[:, :], ps[7][:, :]).then_inc(actT_ready, 1)
                act.wait_ge(down_ready, n + 1)
                act.copy(ys[0][64 * b:64 * b + 64, :], ps[7][0:64, :]).then_inc(ys_ready, 1)
                act.copy(ys[1][64 * b:64 * b + 64, :], ps[7][64:128, :]).then_inc(ys_ready, 1)
                if b == 0:
                    copy_back(pair + 1, 1 - parity)

            def body(it):
                for j in range(TPB):
                    task(it * TPB + j, it * (TPB // 2) + j // 2, j // 2, j % 2)

            act.wait_ge(logits_ready, 1)
            for half in range(2):
                copy_gathered(0, 0, half)
            copy_back(0, 0)
            for half_of_bodies in range(2):
                with act.Fori(BODIES // 2 * half_of_bodies, BODIES // 2 * (half_of_bodies + 1)) as it:
                    body(it)
            act.wait_ge(plan_ready, 1)
            bodies = act.value_load(plan_i[0:1, XCOLS:XCOLS + 1], min_val=0, max_val=XBODIES)
            with act.If(bodies > 0):
                with act.Fori(0, bodies) as xt:
                    body(xt + BODIES)
            load_table(ACT.Sqrt, 6)
            for t in range(NT):
                act.wait_ge(moe_ready, t + 1)
                for half in range(2):
                    squares(2, t, half, square2)
                root(2, t)

        @block.vector
        def _(dve):
            n = [0]

            def step(ins):
                n[0] += 1
                ins.then_inc(dve_step, 1)
                dve.wait_ge(dve_step, n[0])

            def norm(which, t, gain, done):
                dve.wait_ge(squares_summed, 4 * which + (2 * t + 2 if which != 1 else 4))
                dve.scalar_tensor_tensor(out=rstd[:, which, t:t + 1], in0=ss[:, which, t, 0:1], scalar=EPS * D,
                                         in1=ss[:, which, t, 1:2], op0=ALU.add, op1=ALU.add).then_inc(sumsq_ready, 1)
                dve.wait_ge(root_ready, NT * which + t + 1)
                step(dve.reciprocal(rstd[:, which, t:t + 1], rstd[:, which, t:t + 1]))
                dve.scalar_tensor_tensor(out=h_tok[:, t, :], in0=x_res[:, t, :], scalar=rstd[:, which, t:t + 1],
                                         in1=gain[:, :], op0=ALU.mult, op1=ALU.mult).then_inc(done, 1)

            def low_part(c):
                dve.wait_ge(high_ready, c + 1)
                dve.tensor_tensor(w_low[c % NSPLIT][:, :], chunk_in_ring(c), w_high[c % NSPLIT][:, :].bitcast(F32),
                                  ALU.subtract).then_inc(low_ready, 1)

            def read_bank(g, b):
                kind, half, _ = GROUPS[g]
                dve.wait_ge(chunk_used, last_chunk(g) + 1)
                src = group_bank(g, b)[:, :]
                two = src.rearrange("p (m n) -> p m n", m=2)
                m = 4 * half + 2 * b
                if kind == "q":
                    ins = dve.tensor_scalar(qT[:, m:m + 2, :], two, HD ** -0.5, None, ALU.mult)
                elif kind == "cx":
                    dve.wait_ge(bank_read_s, banks_read(group("cc"), b, True))
                    ins = dve.tensor_tensor(u_pad[:, m:m + 2, 2:2 + SEQ], two, cc[:, m:m + 2, :], ALU.mult)
                elif kind == "cb":
                    dve.wait_ge(conv_ready, m + 2)
                    dve.tensor_tensor(conv_s[:, m:m + 2, :], two, conv_s[:, m:m + 2, :], ALU.mult).then_inc(z_ready, 1)
                    dve.wait_ge(zhigh_ready, b + 1)
                    ins = dve.tensor_tensor(zT[1][:, m:m + 2, :], conv_s[:, m:m + 2, :],
                                            zT[0][:, m:m + 2, :].bitcast(F32), ALU.subtract)
                    ins.then_inc(zlow_ready, 1)
                    dve.wait_ge(zlow_ready, b + 1)
                    ins = dve.engine_nop()
                elif kind == "yc":
                    dve.wait_ge(bank_read_s, banks_read(group("gc", half), b, True))
                    ins = dve.tensor_tensor(gate_c[:, m:m + 2, :], two, gate_c[:, m:m + 2, :], ALU.mult)
                elif kind == "ya":
                    dve.wait_ge(bank_read_s, banks_read(group("ga", half), b, True))
                    ins = dve.tensor_tensor(gate_a[:, m:m + 2, :], two, gate_a[:, m:m + 2, :], ALU.mult)
                else:
                    xs = x_res[:, b, 512 * half:512 * half + 512]
                    ins = dve.tensor_tensor(xs, src, xs, ALU.add)
                ins.then_inc(bank_read_v, 1)
                if kind == "ya":
                    dve.wait_ge(bank_read_v, banks_read(g, b, False))
                    dve.tensor_tensor(gate_c[:, m:m + 2, :], gate_c[:, m:m + 2, :], gate_a[:, m:m + 2, :], ALU.add)\
                       .then_inc(merged_ready, 1)
                    dve.wait_ge(mhigh_ready, 2 * half + b + 1)
                    dve.wait_ge(merged_ready, 2 * half + b + 1)
                    dve.tensor_tensor(mT[1][:, m:m + 2, :], gate_c[:, m:m + 2, :], mT[0][:, m:m + 2, :].bitcast(F32),
                                      ALU.subtract).then_inc(mlow_ready, 1)

            dve.wait_ge(gmix_loaded, 16)
            for t in range(NT):
                norm(0, t, g_mix_b, h_ready)
            for i in range(4):
                dve.wait_ge(hT_high, i + 1)
                t, kk = i // 2, i % 2
                k4 = slice(4 * kk, 4 * kk + 4)
                dve.tensor_tensor(hT[1][:, k4, P * t:P * t + P], ps[4 + i][:, :].rearrange("p (k n) -> p k n", k=4),
                                  hT[0][:, k4, P * t:P * t + P].bitcast(F32), ALU.subtract).then_inc(hT_low, 1)
            dve.wait_ge(fl_high_ready, 1)
            dve.tensor_tensor(fl_low[:, :, :], w_fl[:, :, :], fl_high[:, :, :].bitcast(F32), ALU.subtract)\
               .then_inc(fl_low_ready, 1)
            for c in range(NCHUNK + NSPLIT + 1):
                if c < NCHUNK:
                    low_part(c)
                for g, (kind, half, _) in enumerate(GROUPS):
                    if c == last_chunk(g) + NSPLIT and kind not in BY_SCALAR:
                        for b in range(2):
                            read_bank(g, b)
                if c == last_chunk(0) + NSPLIT:
                    dve.wait_ge(forget_ready, 1)
                    step(dve.tensor_tensor(fz[:, :, :], ps[7][:, 0:NT * HEADS].rearrange("p (t h) -> p t h", t=NT),
                                           bf_b[:, :].rearrange("p (a h) -> p a h", a=1)
                                           .broadcast_to([P, NT, HEADS]), ALU.add))
                    step(dve.tensor_scalar(fa[:, :, :], fz[:, :, :], -1.0, None, ALU.mult))
                    dve.tensor_tensor(fa[:, :, :], fa[:, :, :], fz[:, :, :], ALU.max).then_inc(forget_abs, 1)
                    dve.wait_ge(forget_exp, 1)
                    dve.tensor_scalar(fa[:, :, :], fa[:, :, :], 1.0, None, ALU.add).then_inc(forget_exp1, 1)
                    dve.wait_ge(forget_ln, 1)
                    dve.scalar_tensor_tensor(out=logf[:, :, :], in0=fz[:, :, :], scalar=0.0, in1=fa[:, :, :],
                                             op0=ALU.min, op1=ALU.subtract).then_inc(logf_ready, 1)
                if c == CUMSUM_AT + NSPLIT:
                    dve.wait_ge(cumsum_ready, 1)
                    dve.tensor_copy(c_q[:, :, :], ps[7][:, 16:32].rearrange("p (t h) -> p t h", t=NT)).then_inc(cumsum_read, 1)
                    dve.tensor_scalar(neg_c[:, :], ps[7][0:HEADS, 64:64 + SEQ], -1.0, None, ALU.mult).then_inc(cumsum_read, 1)
                    dve.wait_ge(cumsum_read, 2)
                    dve.wait_ge(consts_made, 2)
                h, off = divmod(c - HEAD_0 - NSPLIT, HEAD_STEP)
                if off == 0 and 0 <= h < HEADS:
                    for t in range(NT):
                        u, w = NT * h + t, P * (t + 1)
                        dve.wait_ge(scores_ready, u + 1)
                        dve.scalar_tensor_tensor(out=s_sb[t][:, 0:w], in0=ps[4 + t][:, 0:w], scalar=c_q[:, t, h:h + 1],
                                                 in1=causal[:, 2 * P - w:2 * P], op0=ALU.add, op1=ALU.add)\
                           .then_inc(scores_read, 1)
                        dve.wait_ge(scores_read, u + 1)
                        dve.tensor_reduce(negmax[:, t:t + 1], s_sb[t][:, 0:w], AX.X, ALU.max, negate=True)\
                           .then_inc(negmax_ready, 1)
                h, off = divmod(c - HEAD_0 - NSPLIT - 1, HEAD_STEP)
                if off == 0 and 0 <= h < HEADS:
                    for t in range(NT):
                        u, w = NT * h + t, P * (t + 1)
                        dve.wait_ge(exp_ready, u + 1)
                        step(dve.reciprocal(prec[:, t:t + 1], psum_row[:, t:t + 1]))
                        dve.tensor_scalar(p_sb[t][:, 0:w], p_sb[t][:, 0:w], prec[:, t:t + 1], None, ALU.mult)\
                           .then_inc(probs_ready, 1)
                h, off = divmod(c - HEAD_0 - NSPLIT - 9, HEAD_STEP)
                if off == 0 and 0 <= h < HEADS and h % 2 == 1:
                    dve.wait_ge(ohigh_ready, h // 2 + 1)
                    dve.tensor_tensor(oT[1][:, h // 2, :], ps[7][:, 0:SEQ], oT[0][:, h // 2, :].bitcast(F32),
                                      ALU.subtract).then_inc(olow_ready, 1)
            dve.wait_ge(gffn_loaded, 16)
            for t in range(NT):
                norm(1, t, g_ffn_b, h2_ready)
            for i in (1, 3):
                dve.wait_ge(h_turned, 4 + i + 1)
                t, kk = i // 2, i % 2
                dve.tensor_copy(h2T[:, 4 * kk:4 * kk + 4, P * t:P * t + P],
                                ps[4 + i][:, :].rearrange("p (k n) -> p k n", k=4)).then_inc(h2T_by_vector, 1)
            dve.memset(back[1][:, :], 0.0).then_inc(cleared, 1)
            for b in range(2):
                dve.memset(bsel[b][:, :], 0.0).then_inc(cleared, 1)
            dve.memset(table[:, :, :, E:TCOLS], 0.0).then_inc(cleared, 1)

            dve.wait_ge(logits_ready, 1)
            step(dve.tensor_tensor(logits[:, :, :], ps[7][:, 0:NT * E].rearrange("p (t e) -> p t e", t=NT),
                                   br_b[:, :].rearrange("p (a e) -> p a e", a=1).broadcast_to([P, NT, E]), ALU.add))
            for t in range(NT):
                step(dve.max(top8[:, t, :], logits[:, t, :]))
                dve.tensor_scalar(topn[:, t:t + 1], top8[:, t, 0:1], -1.0, None, ALU.mult).then_inc(top_ready, 1)
                dve.max_index(idx8[:, t, :], top8[:, t, :], logits[:, t, :]).then_inc(index_ready, 1)
            dve.wait_ge(index_ready, NT)
            step(dve.tensor_copy(idxf[:, :, :], idx8[:, :, 0:TOPK]))
            eight = NT * TOPK
            step(dve.tensor_tensor(eq4[:, :, :], iota_f[:, 0:E].rearrange("p (a e) -> p a e", a=1).broadcast_to([P, eight, E]),
                                   idxf[:, :, :].rearrange("p t (k a) -> p (t k) a", a=1).broadcast_to([P, eight, E]),
                                   ALU.is_equal))
            dve.tensor_reduce(chosen[:, :, :], eq4[:, :, :].rearrange("p (t k) e -> p t e k", t=NT), AX.X, ALU.add)\
               .then_inc(chosen_ready, 1)
            dve.wait_ge(gexp_ready, NT)
            step(dve.reciprocal(grec[:, :], gsum[:, :]))
            for t in range(NT):
                step(dve.tensor_scalar(gate4[:, t, :], gexp[:, t, :], grec[:, t:t + 1], None, ALU.mult))
            step(dve.tensor_tensor(eg4[:, :, :], eq4[:, :, :], gate4[:, :, :].rearrange("p t (k a) -> p (t k) a", a=1)
                                   .broadcast_to([P, eight, E]), ALU.mult))
            step(dve.tensor_reduce(table[:, :, 1, 0:E], eg4[:, :, :].rearrange("p (t k) e -> p t e k", t=NT), AX.X, ALU.add))
            dve.wait_ge(rank_ready, 1)
            step(dve.scalar_tensor_tensor(out=table[:, :, 0, 0:E], in0=ps[6][:, 0:NT * E].rearrange("p (t e) -> p t e", t=NT),
                                          scalar=1.0, in1=chosen[:, :, :], op0=ALU.add, op1=ALU.mult))
            step(dve.tensor_scalar(table[:, :, 0, 0:E], table[:, :, 0, 0:E], -1.0, None, ALU.add))
            dve.wait_ge(cleared, 4)

            def make_pick(pair, parity):
                def own(ins, i):
                    ins.then_inc(pick_step, 1)
                    dve.wait_ge(pick_step, pair * (1 + 2 * NT) + i)
                own(dve.tensor_copy(col_now[:, :, :, :], table[:, :, :, bass.ds(pair * 2, 2)]), 1)
                slots = slot_f[:, :].rearrange("p (a s) -> p a s", a=1).broadcast_to([P, 2, CAP])
                for t in range(NT):
                    rank_b, gate_b = (col_now[:, t, c, :].rearrange("p (b a) -> p b a", a=1).broadcast_to([P, 2, CAP])
                                      for c in range(2))
                    own(dve.tensor_tensor(pick[:, t, :].rearrange("p (b s) -> p b s", b=2), slots, rank_b,
                                          ALU.is_equal), 2 + 2 * t)
                    own(dve.tensor_tensor(pickg[:, t, :].rearrange("p (b s) -> p b s", b=2),
                                          pick[:, t, :].rearrange("p (b s) -> p b s", b=2), gate_b, ALU.mult), 3 + 2 * t)
                dve.tensor_copy(bsel[parity][0:E, :].rearrange("p (b s) -> p b s", b=2),
                                tasks[0:E, bass.ds(pair * 2, 2)].rearrange("p (b a) -> p b a", a=1)
                                .broadcast_to([E, 2, CAP])).then_inc(pick_ready, 1)

            make_pick(0, 0)
            dve.tensor_copy(chosen_x[:, :, :], chosen[:, :, :]).then_inc(chosen_kept, 1)
            dve.wait_ge(chosen_kept, 1)
            for b in range(2):
                dve.memset(ys[b][:, :], 0.0).then_inc(ys_ready, 1)
            dve.engine_nop().then_inc(gu_read, 1)

            def task(n_task):
                dve.wait_ge(gu_ready, n_task + 1)
                dve.tensor_scalar(glu[:, :], ps[4][:, :], LIMIT, None, ALU.min).then_inc(glu_clamped, 1)
                dve.tensor_scalar(lin[:, :], ps[5][:, :], LIMIT, -LIMIT, ALU.min, ALU.max).then_inc(gu_read, 1)
                dve.wait_ge(sigmoid_ready, n_task + 1)
                dve.tensor_tensor(swi[:, :], glu[:, :], sig[:, :], ALU.mult).then_inc(swi_ready, 1)
                dve.wait_ge(swi_ready, n_task + 1)
                dve.wait_ge(gu_read, n_task + 2)
                dve.scalar_tensor_tensor(out=act_sb[:, :], in0=lin[:, :], scalar=1.0, in1=swi[:, :], op0=ALU.add, op1=ALU.mult)\
                   .then_inc(act_ready, 1)

            def body(it):
                for q in range(TPB // 2):
                    pair = it * (TPB // 2) + q
                    dve.wait_ge(gathered, pair * 2 + 2)
                    dve.wait_ge(back_turned, pair + 1)
                    make_pick(pair + 1, 1 - q)
                    for b in range(2):
                        task(it * TPB + 2 * q + b)

            with dve.Fori(0, BODIES // 2) as it:
                body(it)

            dve.wait_ge(counts_ready, 1)
            step(dve.tensor_scalar(xneed[:, :], iota_f[0:E, 1:1 + XROUNDS], float(USED), None, ALU.mult))
            step(dve.tensor_scalar(xneed[:, :], xneed[:, :], ps[6][0:E, 128:129], None, ALU.is_lt))
            dve.tensor_reduce(xcount[:, :], xneed[:, :], AX.X, ALU.add).then_inc(xcount_ready, 1)
            dve.wait_ge(route_turned, 1)
            dve.tensor_copy(routeT[:, :, :], ps[7][0:E, :].rearrange("e (c n) -> e c n", c=2)).then_inc(routeT_ready, 1)
            dve.wait_ge(xbase_ready, 1)
            step(dve.tensor_copy(xtot[:, :], ps[6][:, 161:162]))
            step(dve.tensor_copy(xbase[:, :], ps[6][0:E, 160:161]))
            step(dve.tensor_tensor(xend[:, :], xbase[:, :], xcount[:, :], ALU.add))
            step(dve.tensor_scalar(xge[:, :], iota_f[0:E, 0:XCOLS], xbase[:, :], None, ALU.is_ge))
            step(dve.tensor_scalar(xlt[:, :], iota_f[0:E, 0:XCOLS], xend[:, :], None, ALU.is_lt))
            step(dve.tensor_tensor(tasks[0:E, E:TCOLS], xge[:, :], xlt[:, :], ALU.mult))
            step(dve.tensor_scalar(xst[:, :], iota_f[0:E, 0:XCOLS], xbase[:, :], 1.0, ALU.subtract, ALU.add))
            dve.scalar_tensor_tensor(out=xst[:, :], in0=xst[:, :], scalar=float(USED), in1=tasks[0:E, E:TCOLS],
                                     op0=ALU.mult, op1=ALU.mult).then_inc(xtasks_ready, 1)
            step(dve.tensor_scalar(past[:, :], iota_f[:, 0:XCOLS], xtot[:, :], 4096.0, ALU.is_ge, ALU.mult))
            step(dve.tensor_scalar(bodyn[:, :], iota_f[0:1, 0:XBODIES], float(TPB), None, ALU.mult))
            step(dve.tensor_scalar(bodyn[:, :], bodyn[:, :], xtot[0:1, :], None, ALU.is_lt))
            dve.wait_ge(plan_turned, 1)
            step(dve.tensor_tensor(tstart[:, :], ps[6][:, 192:192 + XCOLS], past[:, :], ALU.add))
            step(dve.tensor_reduce(past[0:1, 0:1], bodyn[:, :], AX.X, ALU.add))
            step(dve.tensor_copy(plan_i[:, XCOLS:XCOLS + 1], past[0:1, 0:1]))
            dve.tensor_copy(plan_i[:, 0:XCOLS], ps[6][0:1, 256:256 + XCOLS]).then_inc(plan_ready, 1)
            tab = ps[7][:, 0:NT * 2 * XCOLS].rearrange("p (t c n) -> p t c n", t=NT, c=2)
            for t in range(NT):
                step(dve.tensor_copy(table[:, t, :, E:TCOLS], tab[:, t, :, :]))
                step(dve.tensor_tensor(table[:, t, 0, E:TCOLS], table[:, t, 0, E:TCOLS], tstart[:, :], ALU.subtract))
            dve.engine_nop().then_inc(table_ready, 1)

            with dve.Fori(BODIES // 2, BODIES) as it:
                body(it)
            dve.wait_ge(plan_ready, 1)
            bodies = dve.value_load(plan_i[0:1, XCOLS:XCOLS + 1], min_val=0, max_val=XBODIES)
            with dve.If(bodies > 0):
                with dve.Fori(0, bodies) as xt:
                    body(xt + BODIES)
            for t in range(NT):
                dve.wait_ge(combined, t + 1)
                for half in range(2):
                    xs = x_res[:, t, 512 * half:512 * half + 512]
                    ins = dve.tensor_tensor(xs, ps[2 * t + half][:, :], xs, ALU.add)
                ins.then_inc(moe_ready, 1)
            dve.wait_ge(moe_ready, NT)
            dve.wait_ge(gfinal_loaded, 16)
            for t in range(NT):
                norm(2, t, g_final_b, final_ready)

        @block.tensor
        def _(pe):
            def turn_h(t, ready):
                pe.wait_ge(ready, t + 1)
                for kk in range(2):
                    for k in range(4):
                        c = P * (4 * kk + k)
                        ins = pe.transpose(ps[4 + 2 * t + kk][:, P * k:P * k + P], h_tok[:, t, c:c + P], ident[:, :])
                    ins.then_inc(h_turned, 1)

            def products(c):
                g, k = CHUNKS[c]
                kind = GROUPS[g][0]
                if k == 0 and g >= 2:
                    by_scalar = GROUPS[g - 2][0] in BY_SCALAR
                    pe.wait_ge(bank_read_s if by_scalar else bank_read_v, banks_read(g - 2, 1, by_scalar))
                pe.wait_ge(low_ready, c + 1)
                wh, wl = w_high[c % NSPLIT], w_low[c % NSPLIT]
                a = {"yc": zT, "ya": oT, "x": mT}.get(kind, hT)
                if kind in TOKEN_MAJOR:
                    for t in range(NT):
                        high, low = (part[:, k, P * t:P * t + P] for part in a)
                        for i, (act_part, w_part) in enumerate(((high, wh), (high, wl), (low, wh))):
                            ins = pe.matmul(group_bank(g, t)[:, :], act_part, w_part[:, :], start=(k == 0 and i == 0),
                                            stop=False, skip_group_check=True)
                else:
                    for m in range(4):
                        bank = group_bank(g, m // 2)[:, SEQ * (m % 2):SEQ * (m % 2) + SEQ]
                        cols = slice(P * m, P * m + P)
                        for i, (w_part, act_part) in enumerate(((wh, a[0]), (wh, a[1]), (wl, a[0]))):
                            ins = pe.matmul(bank, w_part[:, cols], act_part[:, k, :],
                                            start=(k == 0 and i == 0 and m % 2 == 0), stop=False, skip_group_check=True)
                ins.then_inc(chunk_used, 1)

            def scores(h):
                m, lo = h // 2, HD * (h % 2)
                for t in range(NT):
                    u, w = NT * h + t, P * (t + 1)
                    if u >= NT:
                        pe.wait_ge(scores_read, u - NT + 1)
                    pe.matmul(ps[4 + t][:, 0:w], qT[lo:lo + HD, m, P * t:P * t + P], kT[lo:lo + HD, m, 0:w],
                              start=True, stop=False)
                    pe.matmul(ps[4 + t][:, 0:w], ident[0:HEADS, h:h + 1].broadcast_to([HEADS, P]), neg_c[:, 0:w],
                              start=False, stop=True).then_inc(scores_ready, 1)

            def turn_probs(h):
                pe.wait_ge(probs_ready, NT * h + NT)
                if h >= 1:
                    pe.wait_ge(probsT_ready, h)
                pe.transpose(ps[6][:, 0:P], p_sb[0][:, 0:P], ident[:, :])
                pe.transpose(ps[6][:, P:2 * P], p_sb[1][:, 0:P], ident[:, :])
                pe.transpose(ps[6][:, 2 * P:3 * P], p_sb[1][:, P:2 * P], ident[:, :]).then_inc(probs_turned, 1)

            def values(h):
                pe.wait_ge(probsT_ready, h + 1)
                if h % 2 == 0 and h >= 2:
                    pe.wait_ge(olow_ready, h // 2)
                lo = HD * (h % 2)
                pe.matmul(ps[7][lo:lo + HD, 0:SEQ], v_tok[:, 0, HD * h:HD * h + HD], pT_sb[:, 0:SEQ],
                          start=True, stop=False, skip_group_check=True)
                pe.matmul(ps[7][lo:lo + HD, P:SEQ], v_tok[:, 1, HD * h:HD * h + HD], pT_sb[:, SEQ:3 * P],
                          start=False, stop=True, skip_group_check=True).then_inc(pv_done, 1)

            pe.wait_ge(consts_made, 1)
            for t in range(NT):
                turn_h(t, h_ready)
            pe.wait_ge(hT_low, 4)
            for c in range(NCHUNK):
                g, k = CHUNKS[c]
                kind, half, _ = GROUPS[g]
                if kind == "yc" and half == 0 and k % 2 == 0:
                    pe.wait_ge(zlow_ready, k // 2 + 1)
                if kind == "ya" and half == 0:
                    pe.wait_ge(olow_ready, k + 1)
                if kind == "x" and half == 0 and k % 2 == 0:
                    pe.wait_ge(mlow_ready, k // 2 + 1)
                products(c)
                if c == last_chunk(0):
                    pe.wait_ge(fl_low_ready, 1)
                    for t in range(NT):
                        for k in range(KD):
                            high, low = (part[:, k, P * t:P * t + P] for part in hT)
                            for i, (a, w) in enumerate(((high, fl_high), (high, fl_low), (low, fl_high))):
                                ins = pe.matmul(ps[7][:, HEADS * t:HEADS * t + HEADS], a, w[:, k, :],
                                                start=(k == 0 and i == 0), stop=(k == KD - 1 and i == 2))
                    ins.then_inc(forget_ready, 1)
                if c == CUMSUM_AT:
                    pe.wait_ge(consts_made, 2)
                    pe.wait_ge(logf_ready, 1)
                    pe.matmul(ps[7][:, 16:24], upto[:, :], logf[:, 0, :], start=True, stop=True)
                    pe.matmul(ps[7][:, 24:32], ones[:, :], logf[:, 0, :], start=True, stop=False)
                    pe.matmul(ps[7][:, 24:32], upto[:, :], logf[:, 1, :], start=False, stop=True)
                    pe.matmul(ps[7][0:HEADS, 64:192], logf[:, 0, :], upto[:, :], start=True, stop=True)
                    pe.matmul(ps[7][0:HEADS, 192:320], logf[:, 0, :], ones[:, :], start=True, stop=False)
                    pe.matmul(ps[7][0:HEADS, 192:320], logf[:, 1, :], upto[:, :], start=False, stop=True)\
                      .then_inc(cumsum_ready, 1)
                h, off = divmod(c - HEAD_0, HEAD_STEP)
                if off == 0 and 0 <= h < HEADS:
                    if h == 0:
                        pe.wait_ge(cumsum_read, 2)
                        pe.wait_ge(bank_read_v, banks_read(group("q"), 1, False))
                        pe.wait_ge(bank_read_s, banks_read(group("k"), 1, True))
                    scores(h)
                h, off = divmod(c - HEAD_0 - 4, HEAD_STEP)
                if off == 0 and 0 <= h < HEADS:
                    turn_probs(h)
                h, off = divmod(c - HEAD_0 - 9, HEAD_STEP)
                if off == 0 and 0 <= h < HEADS:
                    if h == 0:
                        pe.wait_ge(bank_read_s, banks_read(group("v"), 1, True))
                    values(h)

            for t in range(NT):
                turn_h(t, h2_ready)
            pe.wait_ge(h2T_by_scalar, 2)
            pe.wait_ge(h2T_by_vector, 2)
            pe.wait_ge(wrt_loaded, 16)
            for t in range(NT):
                for k in range(KD):
                    ins = pe.matmul(ps[7][:, E * t:E * t + E], h2T[:, k, P * t:P * t + P], w_rt[:, k, :],
                                    start=(k == 0), stop=(k == KD - 1))
            ins.then_inc(logits_ready, 1)
            pe.wait_ge(chosen_ready, 1)
            pe.matmul(ps[6][:, 0:E], below[:, :], chosen[:, 0, :], start=True, stop=True)
            pe.matmul(ps[6][:, E:2 * E], ones[:, :], chosen[:, 0, :], start=True, stop=False)
            pe.matmul(ps[6][:, E:2 * E], below[:, :], chosen[:, 1, :], start=False, stop=True).then_inc(rank_ready, 1)

            def gather(pair, half):
                pe.wait_ge(pick_ready, pair + 1)
                for k in range(4):
                    c = P * (4 * half + k)
                    for t in range(NT):
                        ins = pe.matmul(ps[6][:, P * k:P * k + P], h_tok[:, t, c:c + P], pick[:, t, :],
                                        start=(t == 0), stop=(t == NT - 1))
                ins.then_inc(gathered, 1)

            def turn_back():
                for t in range(NT):
                    ins = pe.transpose(ps[6][:, P * t:P * t + P], pickg[:, t, :], ident[:, :])
                ins.then_inc(back_turned, 1)

            def combine(parity):
                return [[pe.matmul(ps[2 * t + half][:, :], back[parity][:, P * t:P * t + P], ys[half][:, :],
                                   start=False, stop=False, skip_group_check=True) for half in range(2)]
                        for t in range(NT)]

            def gate_up(it, j, b, parity):
                stationary = slice(CAP * b, CAP * b + CAP)
                for k in range(KD + 1):
                    u = MIXER_USES + TASK_USES * j + k
                    if k == 0:
                        lhsT, rows = bsel[parity][:, stationary], bias_gu
                    else:
                        u -= 1
                        pe.wait_ge(slot_loaded[u % NSLOT], it * (16 * TPB * TASK_USES // NSLOT) + 16 * (u // NSLOT + 1))
                        lhsT, rows = xsT[parity][:, k - 1, stationary], ring[:, u % NSLOT, :]
                    for g in range(4):
                        bank, lo = ps[4 + g // 2], 64 * (g % 2)
                        ins = pe.matmul(bank[lo:lo + 64, :], lhsT, rows[:, 512 * g:512 * g + 512],
                                        start=(k == 0), stop=(k == KD))
                    if k > 0:
                        ins.then_inc(slot_freed if k < KD else gu_ready, 1)

            def down(it, j):
                for k in range(KD):
                    u = MIXER_USES + TASK_USES * j + 8 + k // 2
                    if k % 2 == 0:
                        pe.wait_ge(slot_loaded[u % NSLOT], it * (16 * TPB * TASK_USES // NSLOT) + 16 * (u // NSLOT + 1))
                    lo = P * (k % 4) + 64 * (k // 4)
                    w = in_slot(u, 2)[:, k % 2, :]
                    for half in range(2):
                        ins = pe.matmul(ps[7][64 * half:64 * half + 64, :], act_T[:, lo:lo + 64],
                                        w[:, 512 * half:512 * half + 512], start=(k == 0), stop=(k == KD - 1))
                    if k % 2 == 1:
                        ins.then_inc(slot_freed if k < KD - 1 else down_ready, 1)

            def body(it):
                for j in range(TPB):
                    q, b = j // 2, j % 2
                    task, pair = it * TPB + j, it * (TPB // 2) + q
                    if b == 0:
                        pe.wait_ge(xsT_ready, pair * 2 + 2)
                    pe.wait_ge(gu_read, task + 1)
                    gate_up(it, j, b, q)
                    if b == 1:
                        pe.wait_ge(back_ready, pair + 2)
                    gather(pair + 1, b)
                    pe.wait_ge(ys_ready, task * 2 + 2)
                    if b == 0:
                        combine(1 - q)
                    pe.wait_ge(act_ready, task + 1)
                    for c in range(4):
                        ins = pe.transpose(ps[7][:, P * c:P * c + P], act_sb[:, P * c:P * c + P], ident[:, :])
                    ins.then_inc(act_turned, 1)
                    pe.wait_ge(actT_ready, task + 1)
                    down(it, j)
                    if b == 0:
                        pe.wait_ge(xsT_ready, pair * 2 + 3)
                        turn_back()

            pe.wait_ge(cleared, 4)
            for half in range(2):
                if half:
                    pe.wait_ge(xsT_ready, 1)
                gather(0, half)
            pe.wait_ge(ys_ready, 2)
            zero16 = ys[0][:, :].bitcast(BF16)
            for i in range(4):
                pe.matmul(ps[i][:, :], zero16[:, 0:P], zero16[:, 0:512], start=True, stop=False, skip_group_check=True)
            pe.wait_ge(xsT_ready, 2)
            turn_back()
            pe.wait_ge(back_ready, 1)
            pe.wait_ge(bgu_loaded, 16)
            with pe.Fori(0, BODIES // 2) as it:
                body(it)

            pe.wait_ge(xsT_ready, BODIES // 2 * TPB + 2)
            pe.wait_ge(ys_ready, BODIES // 2 * TPB * 2 + 2)
            for t in range(NT):
                ins = pe.matmul(ps[6][0:E, 128:129], chosen_x[:, t, :], ones[:, 0:1], start=(t == 0), stop=(t == 1))
            ins.then_inc(counts_ready, 1)
            for c in range(2):
                for t in range(NT):
                    ins = pe.transpose(ps[7][0:E, SEQ * c + P * t:SEQ * c + P * t + P], table[:, t, c, 0:E], ident[:, :])
            ins.then_inc(route_turned, 1)
            pe.wait_ge(xcount_ready, 1)
            pe.matmul(ps[6][0:E, 160:161], below[0:E, 0:E], xcount[:, :], start=True, stop=True)
            pe.matmul(ps[6][:, 161:162], ones[0:E, :], xcount[:, :], start=True, stop=True).then_inc(xbase_ready, 1)
            pe.wait_ge(routeT_ready, 1)
            pe.wait_ge(bdown_loaded, 16)
            for t in range(NT):
                for half in range(2):
                    pe.matmul(ps[2 * t + half][:, :], routeT[:, 1, P * t:P * t + P],
                              bias_down[:, 512 * half:512 * half + 512], start=False, stop=False, skip_group_check=True)
            pe.wait_ge(xtasks_ready, 1)
            pe.matmul(ps[6][:, 192:192 + XCOLS], ones[0:E, :], xst[:, :], start=True, stop=True)
            for t in range(NT):
                for c in range(2):
                    lo = (2 * t + c) * XCOLS
                    pe.matmul(ps[7][:, lo:lo + XCOLS], routeT[:, c, P * t:P * t + P], tasks[0:E, E:TCOLS],
                              start=True, stop=True)
            pe.matmul(ps[6][0:1, 256:256 + XCOLS], part_f[0:E, :], tasks[0:E, E:TCOLS], start=True, stop=True)\
              .then_inc(plan_turned, 1)
            pe.wait_ge(table_ready, 1)

            with pe.Fori(BODIES // 2, BODIES) as it:
                body(it)
            pe.wait_ge(plan_ready, 1)
            bodies = pe.value_load(plan_i[0:1, XCOLS:XCOLS + 1], min_val=0, max_val=XBODIES)
            with pe.If(bodies > 0):
                with pe.Fori(0, bodies) as xt:
                    body(xt + BODIES)
            pe.wait_ge(ys_ready, bodies * (2 * TPB) + (2 * E + 2))
            for ins in combine(1):
                ins[-1].then_inc(combined, 1)


_INS = ["x", "g_mix", "w_in", "conv_w", "b_f", "w_conv_o", "w_attn_o", "w_out", "g_ffn", "w_router", "b_router",
        "w_gate_up", "b_gate_up", "w_down", "b_down", "g_final"]


def kernel(**inputs):
    import numpy as _np
    import concourse.bacc as _bacc
    from concourse.bass_utils import run_bass_kernel_spmd as _run

    nc = _bacc.Bacc("TRN2", target_bir_lowering=False, num_devices=1)
    arrays, args = {}, []
    for name in _INS:
        a = _np.asarray(inputs[name])
        if name == "conv_w":
            a = a.reshape(3, CONV // P, P).transpose(2, 0, 1)
        a = _np.ascontiguousarray(a)
        arrays[f"in_{name}"] = a
        args.append(nc.dram_tensor(f"in_{name}", a.shape, mybir.dt.from_np(a.dtype), kind="ExternalInput").ap())
    args.append(nc.dram_tensor("out_0", (1, SEQ, D), F32, kind="ExternalOutput").ap())
    build(nc, *args)
    r = _run(nc, [arrays], core_ids=[0])
    return r.results[0]["out_0"]
```

```python
from contextlib import ExitStack

import concourse.bass as bass
from concourse import mybir

P = 128
D = 1024
SEQ = 256
NT = SEQ // P
KD = D // P
CONV = 512
HEADS = 8
HD = 64
ATT = HEADS * HD
E = 32
TOPK = 4
FF = 1024
LIMIT = 7.0
ALPHA = 1.702
EPS = 1e-5
NSLOT = 16
SLOT = 2048
CAP = 64
USED = 64
XROUNDS = SEQ // USED - 1
TPB = 4
BODIES = E // TPB
XTASKS = -(-(SEQ * TOPK // (USED + 1)) // TPB) * TPB
XCOLS = XTASKS + 2
TCOLS = E + XCOLS
XBODIES = XTASKS // TPB
W_IN_GROUPS = 10
MIXER_USES = 2 * W_IN_GROUPS + 2 + 2 + 4
TASK_USES = 12
FREED = TASK_USES - 2
MASKED = -1e30

F32 = mybir.dt.float32
F32R = mybir.dt.float32r
BF16 = mybir.dt.bfloat16
I32 = mybir.dt.int32
U32 = mybir.dt.uint32
ALU = mybir.AluOpType
ACT = mybir.ActivationFunctionType
AX = mybir.AxisListType

GROUPS = [("q", 0, 1536), ("k", 0, 2048), ("cc", 0, 512), ("cx", 0, 1024), ("v", 0, 2560), ("cb", 0, 0),
          ("gc", 0, 3080), ("gc", 1, 3592), ("ga", 0, 4104), ("ga", 1, 4616),
          ("yc", 0, 0), ("yc", 1, 512), ("ya", 0, 0), ("ya", 1, 512), ("x", 0, 0), ("x", 1, 512)]
FORGET_COL = 3072
TOKEN_MAJOR = ("v", "x")
BY_SCALAR = ("k", "v", "cc", "gc", "ga")
PROJ_USE = {"yc": 2 * W_IN_GROUPS, "ya": 2 * W_IN_GROUPS + 2, "x": 2 * W_IN_GROUPS + 4}
CHUNKS = [(g, k) for g, (kind, _, _) in enumerate(GROUPS) for k in range(4 if kind in ("yc", "ya") else KD)]
NCHUNK = len(CHUNKS)
WARM_UP = 36
KEEP_WARM = 6
NSPLIT = 3
HEAD_0, HEAD_STEP = 34, 2
TURN_AT, VALUES_AT = 4, 9
CUMSUM_AT = 18


def group(kind, half=0):
    return [(k, h) for k, h, _ in GROUPS].index((kind, half))


def last_chunk(g):
    return max(c for c in range(NCHUNK) if CHUNKS[c][0] == g)


def use_of(c):
    g, k = CHUNKS[c]
    kind = GROUPS[g][0]
    return PROJ_USE[kind] + k // 2 if kind in PROJ_USE else 2 * g + k // 4


def chunks_done(u):
    return max(c for c in range(NCHUNK) if use_of(c) == u) + 1


def banks_read(g, b, by_scalar):
    return 2 * sum((k in BY_SCALAR) == by_scalar for k, _, _ in GROUPS[:g]) + b + 1


def build(nc, x, g_mix, w_in, conv_w, b_f, w_conv_o, w_attn_o, w_out, g_ffn, g_ffn_cols, w_router,
          b_router, w_gate_up, b_gate_up, w_down, b_down, g_final, out):
    with ExitStack() as ctx:
        def sb(name, shape, dt=F32):
            return ctx.enter_context(nc.sbuf_tensor(name, shape, dt))

        def sem(name):
            return ctx.enter_context(nc.semaphore(name))

        ps = [ctx.enter_context(nc.psum_tensor(f"ps{i}", [P, 512], F32)) for i in range(8)]

        KB = 1024
        arena = sb("arena", [P, 201 * KB // 4])
        base = nc.sbuf_base - 201 * KB
        place, end = {}, base
        for name, size in (("ring", NSLOT * 8), ("x", 8), ("h", 8), ("w", 4), ("hT", 16), ("qk", 8), ("v", 4),
                           ("cc", 4), ("u", 5), ("gc", 8), ("ga", 8)):
            place[name] = end
            end += size * KB
        assert end - base == 201 * KB

        def at(name, where, off, shape, dt=F32):
            return nc.alloc_sbuf_tensor_at(name, shape, dt, offset=place[where] + off)

        ring = at("ring", "ring", 0, [P, NSLOT, SLOT])
        x_res = at("x_res", "x", 0, [P, NT, D])
        h_tok = at("h_tok", "h", 0, [P, NT, D])
        w_high = [at("w_high0", "w", 0, [P, 512], F32R)] + \
            [at(f"w_high{i}", "h", 4 * KB * (i - 1), [P, 512], F32R) for i in (1, 2)]
        w_low = [at("w_low0", "w", 2 * KB, [P, 512], F32R)] + \
            [at(f"w_low{i}", "h", 4 * KB * (i - 1) + 2 * KB, [P, 512], F32R) for i in (1, 2)]
        hT = [at(f"hT{i}", "hT", 8 * KB * i, [P, KD, SEQ], F32R) for i in range(2)]
        mT = [at(f"mT{i}", "hT", 8 * KB * i, [P, KD, SEQ], F32R) for i in range(2)]
        qT = at("qT", "qk", 0, [P, 4, SEQ])
        kT = at("kT", "qk", 4 * KB, [P, 4, SEQ])
        oT = [at(f"oT{i}", "qk", 4 * KB * i, [P, 4, SEQ], F32R) for i in range(2)]
        v_tok = at("v_tok", "v", 0, [P, NT, ATT])
        cc = at("cc", "cc", 0, [P, 4, SEQ])
        u_pad = at("u_pad", "u", 0, [P, 4, SEQ + 2])
        zT = [at("zT0", "cc", 0, [P, 4, SEQ], F32R), at("zT1", "u", 0, [P, 4, SEQ], F32R)]
        g_mix_b = at("g_mix_b", "gc", 0, [P, D])
        conv_s = at("conv_s", "gc", 0, [P, 4, SEQ])
        conv_t = at("conv_t", "gc", 4 * KB, [P, 4, SEQ])
        gate_c = at("gate_c", "gc", 0, [P, KD, SEQ])
        gate_a = at("gate_a", "ga", 0, [P, KD, SEQ])
        square0 = at("square0", "ga", 0, [P, 512])
        square1 = at("square1", "u", 0, [P, 512])
        square2 = at("square2", "cc", 0, [P, 512])
        s_sb = [at(f"s_sb{t}", "ga", 512 * t, [P, P * (t + 1)]) for t in range(NT)]
        p_sb = [[at(f"p_sb{i}{t}", "ga", 1536 * (i + 1) + 512 * t, [P, P * (t + 1)]) for t in range(NT)] for i in range(2)]
        pT_sb = [at(f"pT_sb{i}", "ga", 1536 * (i + 3), [P, 3 * P]) for i in range(2)]
        c_rest = at("c_rest", "ga", 0, [HEADS, SEQ])
        c_mid = at("c_mid", "ga", KB, [HEADS, SEQ], BF16)
        neg_c = at("neg_c", "ga", 1536 * 5, [3 * 32, SEQ], BF16)
        g_ffn_b = at("g_ffn_b", "v", 0, [P, D])
        w_rt = at("w_rt", "u", 3 * KB, [P, KD, E])

        x2T = [at("x2T0", "qk", 4 * KB, [P, 4, SEQ]), at("x2T1", "cc", 0, [P, 4, SEQ])]
        logits = at("logits", "qk", 0, [P, NT, E])
        chosen = at("chosen", "qk", KB, [P, NT, E])
        eq4 = at("eq4", "qk", 2 * KB, [P, NT * TOPK, E])
        eg4 = at("eg4", "qk", 3 * KB, [P, NT * TOPK, E])

        xsT = [at(f"xsT{i}", "hT", 4 * KB * i, [P, KD, P]) for i in range(2)]
        pick = at("pick", "hT", 8 * KB, [P, NT, P])
        pickg = at("pickg", "hT", 9 * KB, [P, NT, P])
        bsel = [at(f"bsel{i}", "hT", 10 * KB + 512 * i, [P, P]) for i in range(2)]
        table = at("table", "hT", 11 * KB, [P, NT, 2, TCOLS])
        chosen_x = at("chosen_x", "hT", 14 * KB, [P, NT, E])
        act_T = at("act_T", "qk", 0, [P, 512])
        ys = [at(f"ys{h}", "qk", 2 * KB + 2 * KB * h, [P, 512]) for h in range(2)]
        sig = at("sig", "qk", 6 * KB, [P, 512])
        glu = at("glu", "v", 0, [P, 512])
        lin = at("lin", "v", 2 * KB, [P, 512])
        routeT = at("routeT", "v", 2 * KB, [E, 2, SEQ])
        xge = at("xge", "v", 0, [E, XCOLS])
        xlt = at("xlt", "v", 256, [E, XCOLS])
        xst = at("xst", "v", 512, [E, XCOLS])
        past = at("past", "v", 768, [P, XCOLS])
        swi = at("swi", "cc", 0, [P, 512])
        act_sb = at("act_sb", "cc", 2 * KB, [P, 512])
        back = [at(f"back{i}", "u", KB * i, [P, SEQ]) for i in range(2)]
        bias_gu = at("bias_gu", "ga", 0, [P, 2 * FF])
        bias_down = at("bias_down", "gc", 0, [E, D])
        g_final_b = at("g_final_b", "gc", 4 * KB, [P, D])

        ident = sb("ident", [P, P])
        causal = sb("causal", [P, 2 * P])
        head_rows = sb("head_rows", [3 * 32, HEADS], BF16)
        upto = sb("upto", [P, P])
        below = sb("below", [P, P])
        ones = sb("ones", [P, P])
        iota_i = sb("iota_i", [P, 64], I32)
        iota_f = sb("iota_f", [P, 64])
        slot_f = sb("slot_f", [P, CAP]) if USED < CAP else iota_f
        part_i = sb("part_i", [P, 1], I32)
        part_f = sb("part_f", [P, 1])
        warm = sb("warm", [P, 8])
        w_fl = sb("w_fl", [P, KD, HEADS])
        fl_high = sb("fl_high", [P, KD, HEADS], F32R)
        fl_low = sb("fl_low", [P, KD, HEADS], F32R)
        taps = sb("taps", [P, 3, 4])
        bf_b = sb("bf_b", [P, HEADS])
        br_b = sb("br_b", [P, E])
        g_ffn_col = sb("g_ffn_col", [P, KD])
        ss = sb("ss", [P, 3, NT, 2])
        rstd = sb("rstd", [P, 3, NT])
        fz = sb("fz", [P, NT, HEADS])
        fa = sb("fa", [P, NT, HEADS])
        logf = sb("logf", [P, NT, HEADS])
        c_q = sb("c_q", [P, NT, HEADS])
        negmax = sb("negmax", [P, NT])
        psum_row = sb("psum_row", [P, NT])
        prec = sb("prec", [P, NT])
        top8 = sb("top8", [P, NT, 8])
        idx8 = sb("idx8", [P, NT, 8], U32)
        idxf = sb("idxf", [P, NT, TOPK])
        topn = sb("topn", [P, NT])
        gexp = sb("gexp", [P, NT, TOPK])
        gsum = sb("gsum", [P, NT])
        grec = sb("grec", [P, NT])
        gate4 = sb("gate4", [P, NT, TOPK])
        tasks = sb("tasks", [P, TCOLS])
        tstart = sb("tstart", [P, XCOLS])
        xneed = sb("xneed", [E, XROUNDS])
        xcount = sb("xcount", [E, 1])
        xbase = sb("xbase", [E, 1])
        xend = sb("xend", [E, 1])
        xtot = sb("xtot", [P, 1])
        bodyn = sb("bodyn", [1, XBODIES])
        plan_i = sb("plan_i", [1, XCOLS + 1], I32)
        col_now = sb("col_now", [P, NT, 2, 2])

        slot_loaded = [sem(f"slot_loaded{s}") for s in range(NSLOT)]
        x_loaded = [sem(f"x_loaded{t}") for t in range(NT)]
        low_ready = sem("low_ready")
        first_low_ready = sem("first_low_ready")
        slot_freed = sem("slot_freed")
        plan_ready = sem("plan_ready")
        final_ready = sem("final_ready")
        out_stored = sem("out_stored")
        pool_step = sem("pool_step")
        warm_made = sem("warm_made")
        consts_made = sem("consts_made")
        small_loaded = sem("small_loaded")
        h_ready = sem("h_ready")
        bank_read_v = sem("bank_read_v")
        conv_ready = sem("conv_ready")
        pv_done = sem("pv_done")
        gffn_loaded = sem("gffn_loaded")
        chunk_used = sem("chunk_used")
        wrt_loaded = sem("wrt_loaded")
        merged_ready = sem("merged_ready")
        bgu_loaded = sem("bgu_loaded")
        mlow_ready = sem("mlow_ready")
        bdown_loaded = sem("bdown_loaded")
        gfinal_loaded = sem("gfinal_loaded")
        gmix_loaded = sem("gmix_loaded")
        squares_summed = sem("squares_summed")
        sumsq_ready = sem("sumsq_ready")
        root_ready = sem("root_ready")
        high_ready = sem("high_ready")
        bank_read_s = sem("bank_read_s")
        h_turned = sem("h_turned")
        hT_high = sem("hT_high")
        fl_high_ready = sem("fl_high_ready")
        zlow_ready = sem("zlow_ready")
        mhigh_ready = sem("mhigh_ready")
        forget_abs = sem("forget_abs")
        forget_exp = sem("forget_exp")
        forget_exp1 = sem("forget_exp1")
        forget_ln = sem("forget_ln")
        negmax_ready = sem("negmax_ready")
        probs_turned = sem("probs_turned")
        exp_ready = sem("exp_ready")
        probsT_ready = sem("probsT_ready")
        ohigh_ready = sem("ohigh_ready")
        x2_turned = sem("x2_turned")
        x2T_by_scalar = sem("x2T_by_scalar")
        rstd_ready = sem("rstd_ready")
        h2_scaled = sem("h2_scaled")
        h2_by_pool = sem("h2_by_pool")
        top_ready = sem("top_ready")
        gexp_ready = sem("gexp_ready")
        gathered = sem("gathered")
        xsT_ready = sem("xsT_ready")
        back_turned = sem("back_turned")
        back_ready = sem("back_ready")
        glu_clamped = sem("glu_clamped")
        sigmoid_ready = sem("sigmoid_ready")
        act_turned = sem("act_turned")
        actT_ready = sem("actT_ready")
        down_ready = sem("down_ready")
        ys_ready = [sem(f"ys_ready{half}") for half in range(2)]
        logits_ready = sem("logits_ready")
        dve_step = sem("dve_step")
        hT_low = sem("hT_low")
        fl_low_ready = sem("fl_low_ready")
        forget_ready = sem("forget_ready")
        logf_ready = sem("logf_ready")
        cumsum_ready = sem("cumsum_ready")
        cumsum_read = sem("cumsum_read")
        neg_c_ready = sem("neg_c_ready")
        scores_ready = sem("scores_ready")
        scores_read = sem("scores_read")
        probs_ready = sem("probs_ready")
        olow_ready = sem("olow_ready")
        x2T_by_vector = sem("x2T_by_vector")
        cleared = sem("cleared")
        index_ready = sem("index_ready")
        chosen_ready = sem("chosen_ready")
        rank_ready = sem("rank_ready")
        pick_step = sem("pick_step")
        pick_ready = sem("pick_ready")
        chosen_kept = sem("chosen_kept")
        gu_read = sem("gu_read")
        gu_ready = sem("gu_ready")
        swi_ready = sem("swi_ready")
        act_ready = sem("act_ready")
        counts_ready = sem("counts_ready")
        xcount_ready = sem("xcount_ready")
        route_turned = sem("route_turned")
        routeT_ready = sem("routeT_ready")
        xbase_ready = sem("xbase_ready")
        xtasks_ready = sem("xtasks_ready")
        plan_turned = sem("plan_turned")
        table_ready = sem("table_ready")
        combined = sem("combined")
        h2_by_vector = sem("h2_by_vector")
        sel_ready = sem("sel_ready")
        router_ready = sem("router_ready")

        w_in_k = w_in.rearrange("(k p) n -> p k n", p=P)
        proj = {"yc": w_conv_o.rearrange("(k p) n -> p k n", p=P), "ya": w_attn_o.rearrange("(k p) n -> p k n", p=P),
                "x": w_out.rearrange("(k p) n -> p k n", p=P)}
        gu_k = w_gate_up.rearrange("e (k p) n -> e p k n", p=P)
        dn_k = w_down.rearrange("e (k p) n -> e p k n", p=P)

        def in_slot(u, k):
            return ring[:, u % NSLOT, :].rearrange("p (k n) -> p k n", k=k)

        def mixer_source(u):
            c = [use_of(c) for c in range(NCHUNK)].index(u)
            g, k = CHUNKS[c]
            kind, _, col = GROUPS[g]
            if kind in PROJ_USE:
                return proj[kind][:, k:k + 2, :]
            return w_in_k[:, k:k + 4, col:col + 512]

        def chunk_in_ring(c):
            g, k = CHUNKS[c]
            kind, _, col = GROUPS[g]
            if kind in PROJ_USE:
                return in_slot(use_of(c), 2)[:, k % 2, col:col + 512]
            return in_slot(use_of(c), 4)[:, k % 4, :]

        def group_bank(g, b):
            return ps[2 * (g % 2) + b]

        def spread(vector, n):
            return vector.rearrange("(a n) -> a n", a=1).broadcast_to([P, n])

        block = ctx.enter_context(nc.Block())

        @block.sync
        def _(sp):
            for t in range(NT):
                sp.dma_start(x_res[:, t, :], x[0, P * t:P * t + P, :]).then_inc(x_loaded[t], 16)
                if t == 1:
                    sp.dma_start(g_mix_b[:, :], spread(g_mix, D)).then_inc(gmix_loaded, 16)
            for u in range(MIXER_USES):
                if u == 2:
                    sp.dma_start(w_fl[:, :, :], w_in_k[:, :, FORGET_COL:FORGET_COL + HEADS]).then_inc(small_loaded, 16)
                    sp.dma_start(bf_b[:, :], spread(b_f, HEADS)).then_inc(small_loaded, 16)
                    sp.dma_start(taps[:, :, :], conv_w).then_inc(small_loaded, 16)
                    sp.dma_start(br_b[:, :], spread(b_router, E)).then_inc(small_loaded, 16)
                if u >= NSLOT:
                    sp.wait_ge(low_ready, chunks_done(u - NSLOT))
                sp.dma_start(in_slot(u, 2 if u >= 2 * W_IN_GROUPS else 4), mixer_source(u)).then_inc(slot_loaded[u % NSLOT], 16)

            def wait_for_slot(it, j, i):
                before = TASK_USES * j + i - NSLOT
                task, use = j + (before - TASK_USES * j) // TASK_USES, before % TASK_USES
                if isinstance(it, int) and TASK_USES * TPB * it + before < 0:
                    sp.wait_ge(low_ready, chunks_done(MIXER_USES + before))
                elif use in (7, TASK_USES - 1):
                    sp.wait_ge(gu_ready if use == 7 else down_ready, it * TPB + (task + 1))
                else:
                    sp.wait_ge(slot_freed, it * (TPB * FREED) + (FREED * task + use + (use < 7)))

            def stream_task(e, it, j):
                for i in range(TASK_USES):
                    u = MIXER_USES + TASK_USES * j + i
                    wait_for_slot(it, j, i)
                    if i < 8:
                        sp.dma_start(ring[:, u % NSLOT, :], gu_k[e, :, i, :]).then_inc(slot_loaded[u % NSLOT], 16)
                    else:
                        sp.dma_start(in_slot(u, 2), dn_k[e, :, 2 * (i - 8):2 * (i - 8) + 2, :])\
                          .then_inc(slot_loaded[u % NSLOT], 16)

            for j in range(TPB):
                stream_task(j, 0, j)
            with sp.Fori(1, BODIES) as it:
                for j in range(TPB):
                    stream_task(it * TPB + j, it, j)
            sp.wait_ge(plan_ready, 1)
            bodies = sp.value_load(plan_i[0:1, XCOLS:XCOLS + 1], min_val=0, max_val=XBODIES)
            with sp.If(bodies > 0):
                with sp.Fori(0, bodies) as xt:
                    for j in range(TPB):
                        e = sp.value_load(plan_i[0:1, bass.ds(xt * TPB + j, 1)], min_val=0, max_val=E - 1)
                        stream_task(e, xt + BODIES, j)
            for t in range(NT):
                for half in range(2):
                    cols = slice(512 * half, 512 * half + 512)
                    sp.wait_ge(final_ready, 2 * t + half + 1)
                    sp.dma_start(out[0, P * t:P * t + P, cols], h_tok[:, t, cols]).then_inc(out_stored, 16)
            sp.wait_ge(out_stored, 16 * 2 * NT)

        @block.gpsimd
        def _(pool):
            n = [0]

            def step(ins):
                n[0] += 1
                ins.then_inc(pool_step, 1)
                pool.wait_ge(pool_step, n[0])

            def all_of(tensor, value):
                step(pool.memset(tensor, value))

            def select(m, op, fill, base, step_x, mult):
                step(pool.affine_select(out=m, in_=m, compare_op=op, fill=fill, base=base,
                                        pattern=[[step_x, P]], channel_multiplier=mult))

            all_of(warm[:, :], 1.0)
            pool.nop().then_inc(warm_made, 1)
            all_of(ident[:, :], 0.0)
            select(ident[:, :], ALU.not_equal, 1.0, 0, -1, 1)
            pool.nop().then_inc(consts_made, 1)
            all_of(ones[:, :], 1.0)
            all_of(upto[:, :], 1.0)
            select(upto[:, :], ALU.is_ge, 0.0, 0, 1, -1)
            all_of(below[:, :], 1.0)
            select(below[:, :], ALU.is_gt, 0.0, 0, 1, -1)
            all_of(causal[:, :], 0.0)
            select(causal[:, P:2 * P], ALU.is_ge, MASKED, 0, -1, 1)
            step(pool.iota(iota_i[:, :], pattern=[[1, 64]], base=0, channel_multiplier=0))
            step(pool.iota(part_i[:, :], pattern=[[0, 1]], base=0, channel_multiplier=1))
            step(pool.tensor_copy(iota_f[:, :], iota_i[:, :]))
            step(pool.tensor_copy(part_f[:, :], part_i[:, :]))
            if USED < CAP:
                step(pool.tensor_copy(slot_f[:, :], iota_f[:, 0:CAP]))
                step(pool.memset(slot_f[:, USED:CAP], 8192.0))
            for m in range(4):
                step(pool.memset(u_pad[:, m, 0:2], 0.0))
            step(pool.memset(tasks[:, :], 0.0))
            step(pool.tensor_copy(tasks[:, 0:E], ident[:, 0:E]))
            pool.nop().then_inc(consts_made, 1)
            step(pool.memset(neg_c[:, :], 0.0))
            step(pool.tensor_copy(head_rows[:, :], ident[0:3 * 32, 0:HEADS]))
            for piece in (1, 2):
                step(pool.tensor_tensor(head_rows[:, :], head_rows[:, :], ident[0:3 * 32, 32 * piece:32 * piece + HEADS], ALU.add))
            pool.nop().then_inc(consts_made, 1)
            pool.wait_ge(high_ready, 1)
            step(pool.tensor_tensor(w_low[0][:, :], chunk_in_ring(0), w_high[0][:, :].bitcast(F32), ALU.subtract))
            pool.nop().then_inc(first_low_ready, 1)
            pool.wait_ge(cumsum_read, 3)
            step(pool.tensor_copy(c_mid[:, :], c_rest[:, :]))
            step(pool.tensor_tensor(c_rest[:, :], c_rest[:, :], c_mid[:, :], ALU.subtract))
            step(pool.tensor_copy(neg_c[32:32 + HEADS, :], c_mid[:, :]))
            pool.tensor_copy(neg_c[64:64 + HEADS, :], c_rest[:, :]).then_inc(neg_c_ready, 1)
            pool.wait_ge(neg_c_ready, 1)
            pool.wait_ge(small_loaded, 16 * 4)
            pool.wait_ge(h_ready, 2 * NT)
            for m in range(4):
                if m % 2 == 0:
                    pool.wait_ge(bank_read_v, banks_read(group("cx"), m // 2, False))
                step(pool.tensor_scalar(conv_s[:, m, :], u_pad[:, m, 0:SEQ], taps[:, 0, m:m + 1], None, ALU.mult))
                for j in (1, 2):
                    step(pool.tensor_scalar(conv_t[:, m, :], u_pad[:, m, j:j + SEQ], taps[:, j, m:m + 1], None, ALU.mult))
                    step(pool.tensor_tensor(conv_s[:, m, :], conv_s[:, m, :], conv_t[:, m, :], ALU.add))
                pool.nop().then_inc(conv_ready, 1)
            for b in range(2):
                m = slice(2 * b, 2 * b + 2)
                pool.wait_ge(bank_read_v, banks_read(group("cb"), b, False))
                step(pool.tensor_copy(zT[0][:, m, :], conv_s[:, m, :]))
                pool.tensor_tensor(zT[1][:, m, :], conv_s[:, m, :], zT[0][:, m, :].bitcast(F32), ALU.subtract)\
                    .then_inc(zlow_ready, 1)
            pool.wait_ge(pv_done, HEADS)
            pool.dma_start(g_ffn_b[:, :], g_ffn.rearrange("(a n) -> a n", a=1).broadcast_to([P, D]))\
                .then_inc(gffn_loaded, 16)
            pool.wait_ge(chunk_used, last_chunk(group("yc", 1)) + 1)
            pool.dma_start(w_rt[:, :, :], w_router.rearrange("(k p) n -> p k n", p=P)).then_inc(wrt_loaded, 16)
            pool.dma_start(g_ffn_col[:, :], g_ffn_cols).then_inc(wrt_loaded, 16)
            for half in range(2):
                for b in range(2):
                    m = 4 * half + 2 * b
                    pool.wait_ge(bank_read_v, banks_read(group("ya", half), b, False))
                    pool.tensor_tensor(gate_c[:, m:m + 2, :], gate_c[:, m:m + 2, :], gate_a[:, m:m + 2, :], ALU.add)\
                        .then_inc(merged_ready, 1)
            pool.wait_ge(merged_ready, 4)
            step(pool.memset(bias_gu[:, :], 0.0))
            pool.dma_start(bias_gu[0:E, :], b_gate_up).then_inc(bgu_loaded, 16)
            pool.wait_ge(wrt_loaded, 16 * 2)
            pool.tensor_tensor(w_rt[:, :, :], w_rt[:, :, :], g_ffn_col[:, :].rearrange("p (k a) -> p k a", a=1)
                               .broadcast_to([P, KD, E]), ALU.mult).then_inc(router_ready, 1)
            pool.wait_ge(mlow_ready, 4)
            pool.dma_start(bias_down[:, :], b_down).then_inc(bdown_loaded, 16)
            pool.dma_start(g_final_b[:, :], g_final.rearrange("(a n) -> a n", a=1).broadcast_to([P, D]))\
                .then_inc(gfinal_loaded, 16)
            pool.wait_ge(squares_summed, 2 * NT * 2)
            pool.memset(back[1][:, :], 0.0).then_inc(cleared, 1)
            for b in range(2):
                pool.memset(bsel[b][:, :], 0.0).then_inc(cleared, 1)
            pool.memset(table[:, :, :, E:TCOLS], 0.0).then_inc(cleared, 1)
            pool.wait_ge(gffn_loaded, 16)
            pool.wait_ge(h2_scaled, 1)
            pool.tensor_tensor(h_tok[:, NT - 1, :], h_tok[:, NT - 1, :], g_ffn_b[:, :], ALU.mult).then_inc(h2_by_pool, 1)

        @block.scalar
        def _(act):
            def load_table(func, i):
                if i == 0:
                    act.wait_ge(warm_made, 1)
                act.activation(warm[:, 1 + i:2 + i], warm[:, 0:1], func)

            def squares(which, t, half, scratch):
                done = 4 * which + (2 * t + half if which != 1 else 2 * half + t)
                if done:
                    act.wait_ge(squares_summed, done)
                row = ps[2 * t + half][:, :] if which == 2 else x_res[:, t, 512 * half:512 * half + 512]
                act.activation(scratch[:, :], row, ACT.Square,
                               accum_out=ss[:, which, t, half:half + 1]).then_inc(squares_summed, 1)

            def root(which, t):
                act.wait_ge(sumsq_ready, NT * which + t + 1)
                act.activation(rstd[:, which, t:t + 1], rstd[:, which, t:t + 1], ACT.Sqrt, scale=1.0 / D)\
                   .then_inc(root_ready, 1)

            def high_part(c):
                if c == 0 or use_of(c) != use_of(c - 1):
                    u = use_of(c)
                    act.wait_ge(slot_loaded[u % NSLOT], 16 * (u // NSLOT + 1))
                if c >= NSPLIT:
                    act.wait_ge(chunk_used, c - NSPLIT + 1)
                act.copy(w_high[c % NSPLIT][:, :], chunk_in_ring(c)).then_inc(high_ready, 1)

            def read_bank(g, b):
                kind, half, _ = GROUPS[g]
                act.wait_ge(chunk_used, last_chunk(g) + 1)
                src = group_bank(g, b)[:, :]
                two = src.rearrange("p (m n) -> p m n", m=2)
                m = 4 * half + 2 * b
                if kind == "k":
                    ins = act.copy(kT[:, m:m + 2, :], two)
                elif kind == "v":
                    ins = act.copy(v_tok[:, b, :], src)
                elif kind == "cc":
                    ins = act.copy(cc[:, m:m + 2, :], two)
                elif kind == "gc":
                    ins = act.activation(gate_c[:, m:m + 2, :], two, ACT.Sigmoid)
                else:
                    ins = act.activation(gate_a[:, m:m + 2, :], two, ACT.Sigmoid)
                ins.then_inc(bank_read_s, 1)

            load_table(ACT.Sqrt, 0)
            for t in range(NT):
                act.wait_ge(x_loaded[t], 16)
                for half in range(2):
                    squares(0, t, half, square0)
                root(0, t)
            for i in range(4):
                act.wait_ge(h_turned, i + 1)
                t, kk = i // 2, i % 2
                act.copy(hT[0][:, 4 * kk:4 * kk + 4, P * t:P * t + P],
                         ps[4 + i][:, :].rearrange("p (k n) -> p k n", k=4)).then_inc(hT_high, 1)
                if i == 1:
                    high_part(0)
            for c in range(1, NCHUNK + NSPLIT + 1):
                if c < NCHUNK:
                    high_part(c)
                if c == 5:
                    act.wait_ge(small_loaded, 16 * 4)
                    act.copy(fl_high[:, :, :], w_fl[:, :, :]).then_inc(fl_high_ready, 1)
                    load_table(ACT.Ln, 1)
                for g, (kind, half, _) in enumerate(GROUPS):
                    if c != last_chunk(g) + NSPLIT:
                        continue
                    if kind in BY_SCALAR:
                        if kind == "gc" and half == 0:
                            act.wait_ge(zlow_ready, 2)
                            load_table(ACT.Sigmoid, 2)
                        if kind == "gc" and half == 1:
                            act.wait_ge(conv_ready, 4)
                        if kind == "ga" and half == 0:
                            act.wait_ge(pv_done, HEADS)
                        for b in range(2):
                            read_bank(g, b)
                        if kind == "ga" and half == 1:
                            load_table(ACT.Sqrt, 3)
                for g, (kind, half, _) in enumerate(GROUPS):
                    late = c - last_chunk(g) - NSPLIT
                    if kind == "ya" and late in (1, 2):
                        b = late - 1
                        m = 4 * half + 2 * b
                        act.wait_ge(merged_ready, 2 * half + b + 1)
                        act.copy(mT[0][:, m:m + 2, :], gate_c[:, m:m + 2, :]).then_inc(mhigh_ready, 1)
                    if kind == "x" and late == 1 - half:
                        for t in range(NT):
                            act.wait_ge(bank_read_v, banks_read(g, t, False))
                            squares(1, t, half, square1)
                if c == last_chunk(group("x", 0)) + 4 + NSPLIT:
                    for t in range(NT):
                        act.wait_ge(x2_turned, t + 1)
                        act.copy(x2T[0][:, :, P * t:P * t + P], ps[4 + t][:, :].rearrange("p (k n) -> p k n", k=4))\
                           .then_inc(x2T_by_scalar, 1)
                if c == last_chunk(0) + NSPLIT:
                    act.wait_ge(forget_abs, 1)
                    act.activation(fa[:, :, :], fa[:, :, :], ACT.Exp, scale=-1.0).then_inc(forget_exp, 1)
                    act.wait_ge(forget_exp1, 1)
                    act.activation(fa[:, :, :], fa[:, :, :], ACT.Ln).then_inc(forget_ln, 1)
                h, off = divmod(c - HEAD_0 - TURN_AT - NSPLIT, HEAD_STEP)
                if off == 0 and 0 <= h < HEADS:
                    act.wait_ge(probs_turned, h + 1)
                    if h >= 2:
                        act.wait_ge(pv_done, h - 1)
                    act.copy(pT_sb[h % 2][:, :], ps[6][:, 0:3 * P]).then_inc(probsT_ready, 1)
                h, off = divmod(c - HEAD_0 - NSPLIT, HEAD_STEP)
                if off == 0 and 0 <= h < HEADS:
                    for t in range(NT):
                        w = P * (t + 1)
                        act.wait_ge(negmax_ready, NT * h + t + 1)
                        if h >= 2:
                            act.wait_ge(probs_turned, h - 1)
                        act.activation(p_sb[h % 2][t][:, 0:w], s_sb[t][:, 0:w], ACT.Exp, bias=negmax[:, t:t + 1],
                                       accum_out=psum_row[:, t:t + 1]).then_inc(exp_ready, 1)
                h, off = divmod(c - HEAD_0 - VALUES_AT - NSPLIT + 1, HEAD_STEP)
                if off == 0 and 0 <= h < HEADS and h % 2 == 1:
                    act.wait_ge(pv_done, h + 1)
                    act.copy(oT[0][:, h // 2, :], ps[7][:, 0:SEQ]).then_inc(ohigh_ready, 1)
            for t in range(NT):
                root(1, t)
            act.wait_ge(rstd_ready, 1)
            act.activation(h_tok[:, NT - 1, :], x_res[:, NT - 1, :], ACT.Copy, scale=rstd[:, 1, NT - 1:NT])\
               .then_inc(h2_scaled, 1)
            load_table(ACT.Exp, 4)
            for t in range(NT):
                act.wait_ge(top_ready, 1)
                act.activation(gexp[:, t, :], top8[:, t, 0:TOPK], ACT.Exp, bias=topn[:, t:t + 1],
                               accum_out=gsum[:, t:t + 1]).then_inc(gexp_ready, 1)
            load_table(ACT.Sigmoid, 5)

            def copy_gathered(pair, parity, half, bank=ps[6]):
                act.wait_ge(gathered, pair * 2 + half + 1)
                act.copy(xsT[parity][:, 4 * half:4 * half + 4, :],
                         bank[:, :].rearrange("p (k n) -> p k n", k=4)).then_inc(xsT_ready, 1)

            def copy_back(pair, parity):
                act.wait_ge(back_turned, pair + 1)
                act.copy(back[parity][:, :], ps[6][:, 0:SEQ]).then_inc(back_ready, 1)

            def task(n, pair, parity, b):
                act.wait_ge(glu_clamped, n + 1)
                act.activation(sig[:, :], glu[:, :], ACT.Sigmoid, scale=ALPHA).then_inc(sigmoid_ready, 1)
                copy_gathered(pair + 1, 1 - parity, b)
                act.wait_ge(act_turned, n + 1)
                act.copy(act_T[:, :], ps[7][:, :]).then_inc(actT_ready, 1)
                act.wait_ge(down_ready, n + 1)
                act.copy(ys[0][64 * b:64 * b + 64, :], ps[7][0:64, :]).then_inc(ys_ready[0], 1)
                if b == 0:
                    copy_back(pair + 1, 1 - parity)

            def body(it):
                for j in range(TPB):
                    task(it * TPB + j, it * (TPB // 2) + j // 2, j // 2, j % 2)

            for half in range(2):
                copy_gathered(0, 0, half, ps[6 + half])
            copy_back(0, 0)
            for half_of_bodies in range(2):
                with act.Fori(BODIES // 2 * half_of_bodies, BODIES // 2 * (half_of_bodies + 1)) as it:
                    body(it)
            act.wait_ge(plan_ready, 1)
            bodies = act.value_load(plan_i[0:1, XCOLS:XCOLS + 1], min_val=0, max_val=XBODIES)
            with act.If(bodies > 0):
                with act.Fori(0, bodies) as xt:
                    body(xt + BODIES)
            load_table(ACT.Sqrt, 6)
            for t in range(NT):
                act.wait_ge(combined, t + 1)
                for half in range(2):
                    squares(2, t, half, square2)
                root(2, t)

        @block.vector
        def _(dve):
            n = [0]

            def step(ins):
                n[0] += 1
                ins.then_inc(dve_step, 1)
                dve.wait_ge(dve_step, n[0])

            def root_of(which, t):
                dve.wait_ge(squares_summed, 4 * which + 2 * t + 2)
                dve.scalar_tensor_tensor(out=rstd[:, which, t:t + 1], in0=ss[:, which, t, 0:1], scalar=EPS * D,
                                         in1=ss[:, which, t, 1:2], op0=ALU.add, op1=ALU.add).then_inc(sumsq_ready, 1)
                dve.wait_ge(root_ready, NT * which + t + 1)
                step(dve.reciprocal(rstd[:, which, t:t + 1], rstd[:, which, t:t + 1]))

            def low_part(c):
                dve.wait_ge(high_ready, c + 1)
                dve.tensor_tensor(w_low[c % NSPLIT][:, :], chunk_in_ring(c), w_high[c % NSPLIT][:, :].bitcast(F32),
                                  ALU.subtract).then_inc(low_ready, 1)

            def read_bank(g, b):
                kind, half, _ = GROUPS[g]
                dve.wait_ge(chunk_used, last_chunk(g) + 1)
                src = group_bank(g, b)[:, :]
                two = src.rearrange("p (m n) -> p m n", m=2)
                m = 4 * half + 2 * b
                if kind == "q":
                    ins = dve.tensor_scalar(qT[:, m:m + 2, :], two, HD ** -0.5, None, ALU.mult)
                elif kind == "cx":
                    dve.wait_ge(bank_read_s, banks_read(group("cc"), b, True))
                    ins = dve.tensor_tensor(u_pad[:, m:m + 2, 2:2 + SEQ], two, cc[:, m:m + 2, :], ALU.mult)
                elif kind == "cb":
                    dve.wait_ge(conv_ready, m + 2)
                    ins = dve.tensor_tensor(conv_s[:, m:m + 2, :], two, conv_s[:, m:m + 2, :], ALU.mult)
                elif kind == "yc":
                    dve.wait_ge(bank_read_s, banks_read(group("gc", half), b, True))
                    ins = dve.tensor_tensor(gate_c[:, m:m + 2, :], two, gate_c[:, m:m + 2, :], ALU.mult)
                elif kind == "ya":
                    dve.wait_ge(bank_read_s, banks_read(group("ga", half), b, True))
                    ins = dve.tensor_tensor(gate_a[:, m:m + 2, :], two, gate_a[:, m:m + 2, :], ALU.mult)
                else:
                    xs = x_res[:, b, 512 * half:512 * half + 512]
                    ins = dve.tensor_tensor(xs, src, xs, ALU.add)
                ins.then_inc(bank_read_v, 1)

            def merged_low(half, b):
                m = 4 * half + 2 * b
                dve.wait_ge(mhigh_ready, 2 * half + b + 1)
                dve.tensor_tensor(mT[1][:, m:m + 2, :], gate_c[:, m:m + 2, :], mT[0][:, m:m + 2, :].bitcast(F32),
                                  ALU.subtract).then_inc(mlow_ready, 1)

            for t in range(NT):
                root_of(0, t)
                dve.wait_ge(gmix_loaded, 16)
                for half in range(2):
                    cols = slice(512 * half, 512 * half + 512)
                    dve.scalar_tensor_tensor(out=h_tok[:, t, cols], in0=x_res[:, t, cols], scalar=rstd[:, 0, t:t + 1],
                                             in1=g_mix_b[:, cols], op0=ALU.mult, op1=ALU.mult).then_inc(h_ready, 1)
            for i in range(4):
                if i == 3:
                    dve.wait_ge(first_low_ready, 1)
                    dve.engine_nop().then_inc(low_ready, 1)
                dve.wait_ge(hT_high, i + 1)
                t, kk = i // 2, i % 2
                k4 = slice(4 * kk, 4 * kk + 4)
                dve.tensor_tensor(hT[1][:, k4, P * t:P * t + P], ps[4 + i][:, :].rearrange("p (k n) -> p k n", k=4),
                                  hT[0][:, k4, P * t:P * t + P].bitcast(F32), ALU.subtract).then_inc(hT_low, 1)
            for c in range(1, NCHUNK + NSPLIT + 1):
                if c < NCHUNK:
                    low_part(c)
                if c == 5:
                    dve.wait_ge(fl_high_ready, 1)
                    dve.tensor_tensor(fl_low[:, :, :], w_fl[:, :, :], fl_high[:, :, :].bitcast(F32), ALU.subtract)\
                       .then_inc(fl_low_ready, 1)
                for g, (kind, half, _) in enumerate(GROUPS):
                    if c == last_chunk(g) + NSPLIT and kind not in BY_SCALAR:
                        for b in range(2):
                            read_bank(g, b)
                    for b in range(2):
                        if kind == "ya" and c == last_chunk(g) + NSPLIT + 1 + b:
                            merged_low(half, b)
                if c == last_chunk(0) + NSPLIT:
                    dve.wait_ge(forget_ready, 1)
                    step(dve.tensor_tensor(fz[:, :, :], ps[7][:, 0:NT * HEADS].rearrange("p (t h) -> p t h", t=NT),
                                           bf_b[:, :].rearrange("p (a h) -> p a h", a=1)
                                           .broadcast_to([P, NT, HEADS]), ALU.add))
                    step(dve.tensor_scalar(fa[:, :, :], fz[:, :, :], -1.0, None, ALU.mult))
                    dve.tensor_tensor(fa[:, :, :], fa[:, :, :], fz[:, :, :], ALU.max).then_inc(forget_abs, 1)
                    dve.wait_ge(forget_exp, 1)
                    dve.tensor_scalar(fa[:, :, :], fa[:, :, :], 1.0, None, ALU.add).then_inc(forget_exp1, 1)
                    dve.wait_ge(forget_ln, 1)
                    dve.scalar_tensor_tensor(out=logf[:, :, :], in0=fz[:, :, :], scalar=0.0, in1=fa[:, :, :],
                                             op0=ALU.min, op1=ALU.subtract).then_inc(logf_ready, 1)
                if c == CUMSUM_AT + NSPLIT:
                    dve.wait_ge(cumsum_ready, 1)
                    dve.tensor_copy(c_q[:, :, :], ps[7][:, 16:32].rearrange("p (t h) -> p t h", t=NT)).then_inc(cumsum_read, 1)
                    dve.wait_ge(consts_made, 3)
                    dve.tensor_scalar(neg_c[0:HEADS, :], ps[7][0:HEADS, 64:64 + SEQ], -1.0, None, ALU.mult).then_inc(cumsum_read, 1)
                    dve.wait_ge(cumsum_read, 2)
                    dve.scalar_tensor_tensor(out=c_rest[:, :], in0=ps[7][0:HEADS, 64:64 + SEQ], scalar=-1.0,
                                             in1=neg_c[0:HEADS, :], op0=ALU.mult, op1=ALU.subtract).then_inc(cumsum_read, 1)
                h, off = divmod(c - HEAD_0 - NSPLIT, HEAD_STEP)
                if off == 0 and 0 <= h < HEADS:
                    for t in range(NT):
                        u, w = NT * h + t, P * (t + 1)
                        dve.wait_ge(scores_ready, u + 1)
                        dve.scalar_tensor_tensor(out=s_sb[t][:, 0:w], in0=ps[4 + t][:, 0:w], scalar=c_q[:, t, h:h + 1],
                                                 in1=causal[:, 2 * P - w:2 * P], op0=ALU.add, op1=ALU.add)\
                           .then_inc(scores_read, 1)
                        dve.wait_ge(scores_read, u + 1)
                        dve.tensor_reduce(negmax[:, t:t + 1], s_sb[t][:, 0:w], AX.X, ALU.max, negate=True)\
                           .then_inc(negmax_ready, 1)
                h, off = divmod(c - HEAD_0 - NSPLIT - 1, HEAD_STEP)
                if off == 0 and 0 <= h < HEADS:
                    for t in range(NT):
                        u, w = NT * h + t, P * (t + 1)
                        dve.wait_ge(exp_ready, u + 1)
                        step(dve.reciprocal(prec[:, t:t + 1], psum_row[:, t:t + 1]))
                        probs = p_sb[h % 2][t][:, 0:w]
                        dve.tensor_scalar(probs, probs, prec[:, t:t + 1], None, ALU.mult)\
                           .then_inc(probs_ready, 1)
                h, off = divmod(c - HEAD_0 - VALUES_AT - NSPLIT + 1, HEAD_STEP)
                if off == 0 and 0 <= h < HEADS and h % 2 == 1:
                    dve.wait_ge(ohigh_ready, h // 2 + 1)
                    dve.tensor_tensor(oT[1][:, h // 2, :], ps[7][:, 0:SEQ], oT[0][:, h // 2, :].bitcast(F32),
                                      ALU.subtract).then_inc(olow_ready, 1)
            for t in range(NT):
                dve.wait_ge(x2_turned, NT + t + 1)
                dve.tensor_copy(x2T[1][:, :, P * t:P * t + P], ps[4 + t][:, :].rearrange("p (k n) -> p k n", k=4))\
                   .then_inc(x2T_by_vector, 1)
            dve.wait_ge(squares_summed, 2 * NT * 2)
            for t in range(NT):
                dve.scalar_tensor_tensor(out=rstd[:, 1, t:t + 1], in0=ss[:, 1, t, 0:1], scalar=EPS * D,
                                         in1=ss[:, 1, t, 1:2], op0=ALU.add, op1=ALU.add).then_inc(sumsq_ready, 1)
            dve.wait_ge(root_ready, 2 * NT)
            dve.reciprocal(rstd[:, 1, :], rstd[:, 1, :]).then_inc(rstd_ready, 1)
            dve.wait_ge(rstd_ready, 1)

            dve.wait_ge(logits_ready, 1)
            for t in range(NT):
                ins = dve.scalar_tensor_tensor(out=logits[:, t, :], in0=ps[7][:, E * t:E * t + E], scalar=rstd[:, 1, t:t + 1],
                                               in1=br_b[:, :], op0=ALU.mult, op1=ALU.add)
            step(ins)
            dve.max(top8[:, 0, :], logits[:, 0, :])
            step(dve.max(top8[:, 1, :], logits[:, 1, :]))
            for t in range(NT):
                dve.max_index(idx8[:, t, :], top8[:, t, :], logits[:, t, :]).then_inc(index_ready, 1)
            dve.tensor_scalar(topn[:, :], top8[:, :, 0], -1.0, None, ALU.mult).then_inc(top_ready, 1)
            dve.wait_ge(index_ready, NT)
            step(dve.tensor_copy(idxf[:, :, :], idx8[:, :, 0:TOPK]))
            eight = NT * TOPK
            step(dve.tensor_tensor(eq4[:, :, :], iota_f[:, 0:E].rearrange("p (a e) -> p a e", a=1).broadcast_to([P, eight, E]),
                                   idxf[:, :, :].rearrange("p t (k a) -> p (t k) a", a=1).broadcast_to([P, eight, E]),
                                   ALU.is_equal))
            dve.tensor_reduce(chosen[:, :, :], eq4[:, :, :].rearrange("p (t k) e -> p t e k", t=NT), AX.X, ALU.add)\
               .then_inc(chosen_ready, 1)
            dve.wait_ge(gffn_loaded, 16)
            for t in range(NT - 1):
                dve.scalar_tensor_tensor(out=h_tok[:, t, :], in0=x_res[:, t, :], scalar=rstd[:, 1, t:t + 1],
                                         in1=g_ffn_b[:, :], op0=ALU.mult, op1=ALU.mult).then_inc(h2_by_vector, 1)
            dve.wait_ge(rank_ready, 1)
            step(dve.scalar_tensor_tensor(out=table[:, :, 0, 0:E], in0=ps[6][:, 0:NT * E].rearrange("p (t e) -> p t e", t=NT),
                                          scalar=1.0, in1=chosen[:, :, :], op0=ALU.add, op1=ALU.mult))
            step(dve.tensor_scalar(table[:, :, 0, 0:E], table[:, :, 0, 0:E], -1.0, None, ALU.add))

            slots = slot_f[:, :].rearrange("p (a s) -> p a s", a=1).broadcast_to([P, 2, CAP])

            def columns(pair, c, i):
                dve.tensor_copy(col_now[:, :, c, :], table[:, :, c, bass.ds(pair * 2, 2)]).then_inc(pick_step, 1)
                dve.wait_ge(pick_step, pair * 2 + i)
                return [col_now[:, t, c, :].rearrange("p (b a) -> p b a", a=1).broadcast_to([P, 2, CAP]) for t in range(NT)]

            def make_pick(pair):
                for t, rank_b in enumerate(columns(pair, 0, 1)):
                    ins = dve.tensor_tensor(pick[:, t, :].rearrange("p (b s) -> p b s", b=2), slots, rank_b, ALU.is_equal)
                ins.then_inc(pick_ready, 1)

            def make_back(pair, parity):
                gates = columns(pair, 1, 2)
                dve.wait_ge(pick_ready, pair + 1)
                for t in range(NT):
                    dve.tensor_tensor(pickg[:, t, :].rearrange("p (b s) -> p b s", b=2),
                                      pick[:, t, :].rearrange("p (b s) -> p b s", b=2), gates[t], ALU.mult)
                dve.tensor_copy(bsel[parity][0:E, :].rearrange("p (b s) -> p b s", b=2),
                                tasks[0:E, bass.ds(pair * 2, 2)].rearrange("p (b a) -> p b a", a=1)
                                .broadcast_to([E, 2, CAP])).then_inc(sel_ready, 1)

            make_pick(0)
            dve.wait_ge(gexp_ready, NT)
            step(dve.reciprocal(grec[:, :], gsum[:, :]))
            for t in range(NT):
                ins = dve.tensor_scalar(gate4[:, t, :], gexp[:, t, :], grec[:, t:t + 1], None, ALU.mult)
            step(ins)
            step(dve.tensor_tensor(eg4[:, :, :], eq4[:, :, :], gate4[:, :, :].rearrange("p t (k a) -> p (t k) a", a=1)
                                   .broadcast_to([P, eight, E]), ALU.mult))
            step(dve.tensor_reduce(table[:, :, 1, 0:E], eg4[:, :, :].rearrange("p (t k) e -> p t e k", t=NT), AX.X, ALU.add))
            dve.wait_ge(cleared, 4)
            make_back(0, 0)
            dve.tensor_copy(chosen_x[:, :, :], chosen[:, :, :]).then_inc(chosen_kept, 1)
            dve.wait_ge(chosen_kept, 1)
            dve.engine_nop().then_inc(gu_read, 1)
            for b in range(2):
                dve.memset(ys[b][:, :], 0.0).then_inc(ys_ready[b], 1)

            def task(n_task, b):
                dve.wait_ge(gu_ready, n_task + 1)
                dve.tensor_scalar(glu[:, :], ps[4][:, :], LIMIT, None, ALU.min).then_inc(glu_clamped, 1)
                dve.tensor_scalar(lin[:, :], ps[5][:, :], LIMIT, -LIMIT, ALU.min, ALU.max).then_inc(gu_read, 1)
                dve.wait_ge(sigmoid_ready, n_task + 1)
                dve.tensor_tensor(swi[:, :], glu[:, :], sig[:, :], ALU.mult).then_inc(swi_ready, 1)
                dve.wait_ge(swi_ready, n_task + 1)
                dve.wait_ge(gu_read, n_task + 2)
                dve.scalar_tensor_tensor(out=act_sb[:, :], in0=lin[:, :], scalar=1.0, in1=swi[:, :], op0=ALU.add, op1=ALU.mult)\
                   .then_inc(act_ready, 1)
                dve.wait_ge(down_ready, n_task + 1)
                dve.tensor_copy(ys[1][64 * b:64 * b + 64, :], ps[7][64:128, :]).then_inc(ys_ready[1], 1)

            def body(it):
                for q in range(TPB // 2):
                    pair = it * (TPB // 2) + q
                    dve.wait_ge(gathered, pair * 2 + 2)
                    dve.wait_ge(back_turned, pair + 1)
                    make_pick(pair + 1)
                    make_back(pair + 1, 1 - q)
                    for b in range(2):
                        task(it * TPB + 2 * q + b, b)

            with dve.Fori(0, BODIES // 2) as it:
                body(it)

            dve.wait_ge(counts_ready, 1)
            step(dve.tensor_scalar(xneed[:, :], iota_f[0:E, 1:1 + XROUNDS], float(USED), None, ALU.mult))
            step(dve.tensor_scalar(xneed[:, :], xneed[:, :], ps[6][0:E, 128:129], None, ALU.is_lt))
            dve.tensor_reduce(xcount[:, :], xneed[:, :], AX.X, ALU.add).then_inc(xcount_ready, 1)
            dve.wait_ge(route_turned, 1)
            dve.tensor_copy(routeT[:, :, :], ps[7][0:E, :].rearrange("e (c n) -> e c n", c=2)).then_inc(routeT_ready, 1)
            dve.wait_ge(xbase_ready, 1)
            step(dve.tensor_copy(xtot[:, :], ps[6][:, 161:162]))
            step(dve.tensor_copy(xbase[:, :], ps[6][0:E, 160:161]))
            step(dve.tensor_tensor(xend[:, :], xbase[:, :], xcount[:, :], ALU.add))
            step(dve.tensor_scalar(xge[:, :], iota_f[0:E, 0:XCOLS], xbase[:, :], None, ALU.is_ge))
            step(dve.tensor_scalar(xlt[:, :], iota_f[0:E, 0:XCOLS], xend[:, :], None, ALU.is_lt))
            step(dve.tensor_tensor(tasks[0:E, E:TCOLS], xge[:, :], xlt[:, :], ALU.mult))
            step(dve.tensor_scalar(xst[:, :], iota_f[0:E, 0:XCOLS], xbase[:, :], 1.0, ALU.subtract, ALU.add))
            dve.scalar_tensor_tensor(out=xst[:, :], in0=xst[:, :], scalar=float(USED), in1=tasks[0:E, E:TCOLS],
                                     op0=ALU.mult, op1=ALU.mult).then_inc(xtasks_ready, 1)
            step(dve.tensor_scalar(past[:, :], iota_f[:, 0:XCOLS], xtot[:, :], 4096.0, ALU.is_ge, ALU.mult))
            step(dve.tensor_scalar(bodyn[:, :], iota_f[0:1, 0:XBODIES], float(TPB), None, ALU.mult))
            step(dve.tensor_scalar(bodyn[:, :], bodyn[:, :], xtot[0:1, :], None, ALU.is_lt))
            dve.wait_ge(plan_turned, 1)
            step(dve.tensor_tensor(tstart[:, :], ps[6][:, 192:192 + XCOLS], past[:, :], ALU.add))
            step(dve.tensor_reduce(past[0:1, 0:1], bodyn[:, :], AX.X, ALU.add))
            step(dve.tensor_copy(plan_i[:, XCOLS:XCOLS + 1], past[0:1, 0:1]))
            dve.tensor_copy(plan_i[:, 0:XCOLS], ps[6][0:1, 256:256 + XCOLS]).then_inc(plan_ready, 1)
            tab = ps[7][:, 0:NT * 2 * XCOLS].rearrange("p (t c n) -> p t c n", t=NT, c=2)
            for t in range(NT):
                step(dve.tensor_copy(table[:, t, :, E:TCOLS], tab[:, t, :, :]))
                step(dve.tensor_tensor(table[:, t, 0, E:TCOLS], table[:, t, 0, E:TCOLS], tstart[:, :], ALU.subtract))
            dve.engine_nop().then_inc(table_ready, 1)

            with dve.Fori(BODIES // 2, BODIES) as it:
                body(it)
            dve.wait_ge(plan_ready, 1)
            bodies = dve.value_load(plan_i[0:1, XCOLS:XCOLS + 1], min_val=0, max_val=XBODIES)
            with dve.If(bodies > 0):
                with dve.Fori(0, bodies) as xt:
                    body(xt + BODIES)
            dve.wait_ge(gfinal_loaded, 16)
            for t in range(NT):
                root_of(2, t)
                for half in range(2):
                    cols = slice(512 * half, 512 * half + 512)
                    dve.scalar_tensor_tensor(out=h_tok[:, t, cols], in0=ps[2 * t + half][:, :], scalar=rstd[:, 2, t:t + 1],
                                             in1=g_final_b[:, cols], op0=ALU.mult, op1=ALU.mult).then_inc(final_ready, 1)

        @block.tensor
        def _(pe):
            def turn_h(t):
                for kk in range(2):
                    pe.wait_ge(h_ready, 2 * t + kk + 1)
                    for k in range(4):
                        c = P * (4 * kk + k)
                        ins = pe.transpose(ps[4 + 2 * t + kk][:, P * k:P * k + P], h_tok[:, t, c:c + P], ident[:, :])
                    ins.then_inc(h_turned, 1)

            def products(c):
                g, k = CHUNKS[c]
                kind = GROUPS[g][0]
                if k == 0 and g >= 2:
                    by_scalar = GROUPS[g - 2][0] in BY_SCALAR
                    pe.wait_ge(bank_read_s if by_scalar else bank_read_v, banks_read(g - 2, 1, by_scalar))
                pe.wait_ge(low_ready, c + 1)
                wh, wl = w_high[c % NSPLIT], w_low[c % NSPLIT]
                a = {"yc": zT, "ya": oT, "x": mT}.get(kind, hT)
                if kind in TOKEN_MAJOR:
                    for t in range(NT):
                        high, low = (part[:, k, P * t:P * t + P] for part in a)
                        for i, (act_part, w_part) in enumerate(((high, wh), (high, wl), (low, wh))):
                            ins = pe.matmul(group_bank(g, t)[:, :], act_part, w_part[:, :], start=(k == 0 and i == 0),
                                            stop=False, skip_group_check=True)
                else:
                    for m in range(4):
                        bank = group_bank(g, m // 2)[:, SEQ * (m % 2):SEQ * (m % 2) + SEQ]
                        cols = slice(P * m, P * m + P)
                        for i, (w_part, act_part) in enumerate(((wh, a[0]), (wh, a[1]), (wl, a[0]))):
                            ins = pe.matmul(bank, w_part[:, cols], act_part[:, k, :],
                                            start=(k == 0 and i == 0 and m % 2 == 0), stop=False, skip_group_check=True)
                ins.then_inc(chunk_used, 1)

            def scores(h):
                m, lo = h // 2, HD * (h % 2)
                for t in range(NT):
                    u, w = NT * h + t, P * (t + 1)
                    if u >= NT:
                        pe.wait_ge(scores_read, u - NT + 1)
                    pe.matmul(ps[4 + t][:, 0:w], qT[lo:lo + HD, m, P * t:P * t + P], kT[lo:lo + HD, m, 0:w],
                              start=True, stop=False)
                    pe.matmul(ps[4 + t][:, 0:w], head_rows[:, h:h + 1].broadcast_to([3 * 32, P]), neg_c[:, 0:w],
                              start=False, stop=True).then_inc(scores_ready, 1)

            def turn_probs(h):
                pe.wait_ge(probs_ready, NT * h + NT)
                if h >= 1:
                    pe.wait_ge(probsT_ready, h)
                pe.transpose(ps[6][:, 0:P], p_sb[h % 2][0][:, 0:P], ident[:, :])
                pe.transpose(ps[6][:, P:2 * P], p_sb[h % 2][1][:, 0:P], ident[:, :])
                pe.transpose(ps[6][:, 2 * P:3 * P], p_sb[h % 2][1][:, P:2 * P], ident[:, :]).then_inc(probs_turned, 1)

            def values(h):
                pe.wait_ge(probsT_ready, h + 1)
                if h % 2 == 0 and h >= 2:
                    pe.wait_ge(olow_ready, h // 2)
                lo = HD * (h % 2)
                pe.matmul(ps[7][lo:lo + HD, 0:SEQ], v_tok[:, 0, HD * h:HD * h + HD], pT_sb[h % 2][:, 0:SEQ],
                          start=True, stop=False, skip_group_check=True)
                pe.matmul(ps[7][lo:lo + HD, P:SEQ], v_tok[:, 1, HD * h:HD * h + HD], pT_sb[h % 2][:, SEQ:3 * P],
                          start=False, stop=True, skip_group_check=True).then_inc(pv_done, 1)

            def turn_x2(t, half):
                pe.wait_ge(bank_read_v, banks_read(group("x", half), t, False))
                for k in range(4):
                    c = P * (4 * half + k)
                    ins = pe.transpose(ps[4 + t][:, P * k:P * k + P], x_res[:, t, c:c + P], ident[:, :])
                ins.then_inc(x2_turned, 1)

            def logits_part(t, half):
                for k in range(4):
                    ins = pe.matmul(ps[7][:, E * t:E * t + E], x2T[half][:, k, P * t:P * t + P], w_rt[:, 4 * half + k, :],
                                    start=(half == 0 and t == 0 and k == 0), stop=False, skip_group_check=True)
                return ins

            def start_sum(i):
                t, half = i // 2, i % 2
                pe.matmul(ps[i][:, :], ident[:, :], x_res[:, t, 512 * half:512 * half + 512],
                          start=True, stop=False, skip_group_check=True)

            def stay_warm(bank, count):
                any16 = ident[:, :].bitcast(BF16)
                for _ in range(count):
                    pe.matmul(bank[:, 0:2 * P], any16[:, 0:P], any16[:, :], start=True, stop=True)

            pe.wait_ge(consts_made, 1)
            stay_warm(ps[0], WARM_UP)
            for t in range(NT):
                turn_h(t)
            stay_warm(ps[2], 8)
            for c in range(NCHUNK):
                g, k = CHUNKS[c]
                if c in (0, KD // 2):
                    pe.wait_ge(hT_low, 3 if c == 0 else 4)
                kind, half, _ = GROUPS[g]
                if kind == "yc" and half == 0 and k % 2 == 0:
                    pe.wait_ge(zlow_ready, k // 2 + 1)
                if kind == "ya" and half == 0:
                    pe.wait_ge(olow_ready, k + 1)
                if kind == "x" and half == 0 and k % 2 == 0:
                    pe.wait_ge(mlow_ready, k // 2 + 1)
                products(c)
                if c == last_chunk(group("x", 0)) + 4:
                    for t in range(NT):
                        turn_x2(t, 0)
                if c == last_chunk(group("x", 0)) + 7:
                    pe.wait_ge(x2T_by_scalar, NT)
                    pe.wait_ge(router_ready, 1)
                    for t in range(NT):
                        logits_part(t, 0)
                if c == last_chunk(0):
                    pe.wait_ge(fl_low_ready, 1)
                    for t in range(NT):
                        for k in range(KD):
                            high, low = (part[:, k, P * t:P * t + P] for part in hT)
                            for i, (a, w) in enumerate(((high, fl_high), (high, fl_low), (low, fl_high))):
                                ins = pe.matmul(ps[7][:, HEADS * t:HEADS * t + HEADS], a, w[:, k, :],
                                                start=(k == 0 and i == 0), stop=(k == KD - 1 and i == 2))
                    ins.then_inc(forget_ready, 1)
                if c == CUMSUM_AT:
                    pe.wait_ge(consts_made, 2)
                    pe.wait_ge(logf_ready, 1)
                    pe.matmul(ps[7][:, 16:24], upto[:, :], logf[:, 0, :], start=True, stop=True)
                    pe.matmul(ps[7][:, 24:32], ones[:, :], logf[:, 0, :], start=True, stop=False)
                    pe.matmul(ps[7][:, 24:32], upto[:, :], logf[:, 1, :], start=False, stop=True)
                    pe.matmul(ps[7][0:HEADS, 64:192], logf[:, 0, :], upto[:, :], start=True, stop=True)
                    pe.matmul(ps[7][0:HEADS, 192:320], logf[:, 0, :], ones[:, :], start=True, stop=False)
                    pe.matmul(ps[7][0:HEADS, 192:320], logf[:, 1, :], upto[:, :], start=False, stop=True)\
                      .then_inc(cumsum_ready, 1)
                h, off = divmod(c - HEAD_0, HEAD_STEP)
                if off == 0 and 0 <= h < HEADS:
                    if h == 0:
                        pe.wait_ge(cumsum_read, 3)
                        pe.wait_ge(neg_c_ready, 1)
                        pe.wait_ge(bank_read_v, banks_read(group("q"), 1, False))
                        pe.wait_ge(bank_read_s, banks_read(group("k"), 1, True))
                    scores(h)
                h, off = divmod(c - HEAD_0 - TURN_AT, HEAD_STEP)
                if off == 0 and 0 <= h < HEADS:
                    turn_probs(h)
                h, off = divmod(c - HEAD_0 - VALUES_AT, HEAD_STEP)
                if off == 0 and 0 <= h < HEADS:
                    if h == 0:
                        pe.wait_ge(bank_read_s, banks_read(group("v"), 1, True))
                    values(h)

            for t in range(NT):
                turn_x2(t, 1)
            for t in range(NT):
                pe.wait_ge(x2T_by_vector, t + 1)
                ins = logits_part(t, 1)
            ins.then_inc(logits_ready, 1)
            for i in range(3):
                start_sum(i)
            pe.wait_ge(chosen_ready, 1)
            pe.matmul(ps[6][:, 0:E], below[:, :], chosen[:, 0, :], start=True, stop=True)
            pe.matmul(ps[6][:, E:2 * E], ones[:, :], chosen[:, 0, :], start=True, stop=False)
            pe.matmul(ps[6][:, E:2 * E], below[:, :], chosen[:, 1, :], start=False, stop=True).then_inc(rank_ready, 1)

            def gather(pair, half, bank=ps[6]):
                pe.wait_ge(pick_ready, pair + 1)
                for k in range(4):
                    c = P * (4 * half + k)
                    for t in range(NT):
                        ins = pe.matmul(bank[:, P * k:P * k + P], h_tok[:, t, c:c + P], pick[:, t, :],
                                        start=(t == 0), stop=(t == NT - 1))
                ins.then_inc(gathered, 1)

            def turn_back(pair):
                pe.wait_ge(sel_ready, pair + 1)
                for t in range(NT):
                    ins = pe.transpose(ps[6][:, P * t:P * t + P], pickg[:, t, :], ident[:, :])
                ins.then_inc(back_turned, 1)

            def combine(parity):
                return [[pe.matmul(ps[2 * t + half][:, :], back[parity][:, P * t:P * t + P], ys[half][:, :],
                                   start=False, stop=False, skip_group_check=True) for half in range(2)]
                        for t in range(NT)]

            def gate_up(it, j, b, parity, pair):
                stationary = slice(CAP * b, CAP * b + CAP)
                for k in range(KD):
                    if b == 0 and k % 4 == 0:
                        pe.wait_ge(xsT_ready, pair * 2 + (k // 4 + 1))
                    u = MIXER_USES + TASK_USES * j + k
                    pe.wait_ge(slot_loaded[u % NSLOT], it * (16 * TPB * TASK_USES // NSLOT) + 16 * (u // NSLOT + 1))
                    for g in range(4):
                        bank, lo = ps[4 + g // 2], 64 * (g % 2)
                        ins = pe.matmul(bank[lo:lo + 64, :], xsT[parity][:, k, stationary],
                                        ring[:, u % NSLOT, 512 * g:512 * g + 512], start=(k == 0), stop=(k == KD - 1))
                    ins.then_inc(slot_freed if k < KD - 1 else gu_ready, 1)
                    if k == KD // 2 - 1:
                        for g in range(4):
                            bank, lo = ps[4 + g // 2], 64 * (g % 2)
                            pe.matmul(bank[lo:lo + 64, :], bsel[parity][:, stationary],
                                      bias_gu[:, 512 * g:512 * g + 512], start=False, stop=False)

            def down(it, j):
                for k in range(KD):
                    u = MIXER_USES + TASK_USES * j + 8 + k // 2
                    if k % 2 == 0:
                        pe.wait_ge(slot_loaded[u % NSLOT], it * (16 * TPB * TASK_USES // NSLOT) + 16 * (u // NSLOT + 1))
                    lo = P * (k % 4) + 64 * (k // 4)
                    w = in_slot(u, 2)[:, k % 2, :]
                    for half in range(2):
                        ins = pe.matmul(ps[7][64 * half:64 * half + 64, :], act_T[:, lo:lo + 64],
                                        w[:, 512 * half:512 * half + 512], start=(k == 0), stop=(k == KD - 1))
                    if k % 2 == 1:
                        ins.then_inc(slot_freed if k < KD - 1 else down_ready, 1)

            def body(it):
                for j in range(TPB):
                    q, b = j // 2, j % 2
                    task, pair = it * TPB + j, it * (TPB // 2) + q
                    pe.wait_ge(gu_read, task + 1)
                    gate_up(it, j, b, q, pair)
                    pe.wait_ge(back_ready, pair + 1 + b)
                    gather(pair + 1, b)
                    for half in range(2):
                        pe.wait_ge(ys_ready[half], task + 1)
                    if b == 0:
                        combine(1 - q)
                    else:
                        stay_warm(ps[7], KEEP_WARM)
                    pe.wait_ge(act_ready, task + 1)
                    for c in range(4):
                        ins = pe.transpose(ps[7][:, P * c:P * c + P], act_sb[:, P * c:P * c + P], ident[:, :])
                    ins.then_inc(act_turned, 1)
                    pe.wait_ge(actT_ready, task + 1)
                    down(it, j)
                    if b == 0:
                        pe.wait_ge(xsT_ready, pair * 2 + 3)
                        turn_back(pair + 1)

            start_sum(3)
            pe.wait_ge(cleared, 4)
            pe.wait_ge(h2_by_vector, 1)
            pe.wait_ge(h2_by_pool, 1)
            for half in range(2):
                gather(0, half, ps[6 + half])
            pe.wait_ge(xsT_ready, 1)
            turn_back(0)
            pe.wait_ge(bgu_loaded, 16)
            with pe.Fori(0, BODIES // 2) as it:
                body(it)

            pe.wait_ge(xsT_ready, BODIES // 2 * TPB + 2)
            for half in range(2):
                pe.wait_ge(ys_ready[half], BODIES // 2 * TPB + 1)
            for t in range(NT):
                ins = pe.matmul(ps[6][0:E, 128:129], chosen_x[:, t, :], ones[:, 0:1], start=(t == 0), stop=(t == 1))
            ins.then_inc(counts_ready, 1)
            for c in range(2):
                for t in range(NT):
                    ins = pe.transpose(ps[7][0:E, SEQ * c + P * t:SEQ * c + P * t + P], table[:, t, c, 0:E], ident[:, :])
            ins.then_inc(route_turned, 1)
            pe.wait_ge(xcount_ready, 1)
            pe.matmul(ps[6][0:E, 160:161], below[0:E, 0:E], xcount[:, :], start=True, stop=True)
            pe.matmul(ps[6][:, 161:162], ones[0:E, :], xcount[:, :], start=True, stop=True).then_inc(xbase_ready, 1)
            pe.wait_ge(routeT_ready, 1)
            pe.wait_ge(bdown_loaded, 16)
            for t in range(NT):
                for half in range(2):
                    pe.matmul(ps[2 * t + half][:, :], routeT[:, 1, P * t:P * t + P],
                              bias_down[:, 512 * half:512 * half + 512], start=False, stop=False, skip_group_check=True)
            pe.wait_ge(xtasks_ready, 1)
            pe.matmul(ps[6][:, 192:192 + XCOLS], ones[0:E, :], xst[:, :], start=True, stop=True)
            for t in range(NT):
                for c in range(2):
                    lo = (2 * t + c) * XCOLS
                    pe.matmul(ps[7][:, lo:lo + XCOLS], routeT[:, c, P * t:P * t + P], tasks[0:E, E:TCOLS],
                              start=True, stop=True)
            pe.matmul(ps[6][0:1, 256:256 + XCOLS], part_f[0:E, :], tasks[0:E, E:TCOLS], start=True, stop=True)\
              .then_inc(plan_turned, 1)
            pe.wait_ge(table_ready, 1)

            with pe.Fori(BODIES // 2, BODIES) as it:
                body(it)
            pe.wait_ge(plan_ready, 1)
            bodies = pe.value_load(plan_i[0:1, XCOLS:XCOLS + 1], min_val=0, max_val=XBODIES)
            with pe.If(bodies > 0):
                with pe.Fori(0, bodies) as xt:
                    body(xt + BODIES)
            for half in range(2):
                pe.wait_ge(ys_ready[half], bodies * TPB + (E + 1))
            for ins in combine(1):
                ins[-1].then_inc(combined, 1)


_INS = ["x", "g_mix", "w_in", "conv_w", "b_f", "w_conv_o", "w_attn_o", "w_out", "g_ffn", "g_ffn_cols", "w_router",
        "b_router", "w_gate_up", "b_gate_up", "w_down", "b_down", "g_final"]


def kernel(**inputs):
    import numpy as _np
    import concourse.bacc as _bacc
    from concourse.bass_utils import run_bass_kernel_spmd as _run

    nc = _bacc.Bacc("TRN2", target_bir_lowering=False, num_devices=1)
    arrays, args = {}, []
    for name in _INS:
        a = _np.asarray(inputs["g_ffn" if name == "g_ffn_cols" else name])
        if name == "g_ffn_cols":
            a = a.reshape(KD, P).T
        if name == "conv_w":
            a = a.reshape(3, CONV // P, P).transpose(2, 0, 1)
        a = _np.ascontiguousarray(a)
        arrays[f"in_{name}"] = a
        args.append(nc.dram_tensor(f"in_{name}", a.shape, mybir.dt.from_np(a.dtype), kind="ExternalInput").ap())
    args.append(nc.dram_tensor("out_0", (1, SEQ, D), F32, kind="ExternalOutput").ap())
    build(nc, *args)
    r = _run(nc, [arrays], core_ids=[0])
    return r.results[0]["out_0"]
```
